# Optimizing a Trainium2 kernel written in Bass

```python
import jax, jax.numpy as jnp
from jax import lax
import numpy as np

D_MODEL = 1024
BATCH = 1
SEQ = 512
DEPTH = 1

D_MIX = D_MODEL
GDN_HEADS = 4
GDN_DK = 128
GDN_DV = 128
GDN_CONV = 4
GDN_CHUNK = 64
NSA_HEADS = 8
NSA_KV = 2
NSA_DH = 64
CMP_BLOCK = 32
CMP_STRIDE = 16
CMP_HIDDEN = 128
SEL_BLOCK = 64
SEL_TOPK = 16
WINDOW = 512
SEL_QCHUNK = 32
WIN_QBLOCK = 128
ROPE_THETA = 500000.0
ROPE_DIM = NSA_DH // 4
D_FF = 2816
EPS = 1e-6
NEG = -1e30
BIG = 1e30

W_GDN_QKV = GDN_HEADS * (2 * GDN_DK + GDN_DV)
W_GDN_Z = GDN_HEADS * GDN_DV
W_GDN_A = GDN_HEADS
W_GDN_B = GDN_HEADS
W_NSA_Q = NSA_HEADS * NSA_DH
W_NSA_KV = 2 * NSA_KV * NSA_DH
W_NSA_GATE = 3 * NSA_HEADS
D_IN = W_GDN_QKV + W_GDN_Z + W_GDN_A + W_GDN_B + W_NSA_Q + 3 * W_NSA_KV + W_NSA_GATE

kernel_name = "hybrid_gdn_nsa_macaron_block"

def rmsnorm(x, w):
    xf = x.astype(jnp.float32)
    y = xf * lax.rsqrt(jnp.mean(xf * xf, axis=-1, keepdims=True) + EPS)
    return (y * w.astype(jnp.float32)).astype(x.dtype)

def l2norm(x):
    xf = x.astype(jnp.float32)
    return xf * lax.rsqrt(jnp.sum(xf * xf, axis=-1, keepdims=True) + EPS)

def swiglu(x, w_gate, w_up, w_down):
    return (jax.nn.silu(x @ w_gate) * (x @ w_up)) @ w_down

def split_cols(y, widths):
    cuts = np.cumsum(widths)[:-1].tolist()
    return jnp.split(y, cuts, axis=-1)

def masked_softmax(s, mask):
    s = jnp.where(mask, s.astype(jnp.float32), NEG)
    m = jnp.max(s, axis=-1, keepdims=True)
    p = jnp.exp(s - m) * mask
    return p / jnp.maximum(jnp.sum(p, axis=-1, keepdims=True), 1e-30)

def partial_rope(x, pos):
    half = ROPE_DIM // 2
    inv = ROPE_THETA ** (-jnp.arange(half, dtype=jnp.float32) / half)
    ang = pos.astype(jnp.float32)[:, None] * inv[None, :]
    cos = jnp.cos(ang)[None, :, None, :]
    sin = jnp.sin(ang)[None, :, None, :]
    xr = x[..., :ROPE_DIM].astype(jnp.float32)
    x1, x2 = xr[..., :half], xr[..., half:]
    rot = jnp.concatenate([x1 * cos - x2 * sin, x2 * cos + x1 * sin], axis=-1).astype(x.dtype)
    return jnp.concatenate([rot, x[..., ROPE_DIM:]], axis=-1)

def causal_depthwise_conv(x, w):
    k = w.shape[0]
    return lax.conv_general_dilated(
        x, w[:, None, :].astype(x.dtype), window_strides=(1,), padding=[(k - 1, 0)],
        dimension_numbers=("NWC", "WIO", "NWC"), feature_group_count=x.shape[-1])

def gated_delta_chunked(q, k, v, g, beta):
    bsz, s_len, h, dk = q.shape
    dv = v.shape[-1]
    c = GDN_CHUNK
    n = s_len // c
    q = q.astype(jnp.float32) * (dk ** -0.5)
    k = k.astype(jnp.float32)
    v = v.astype(jnp.float32)

    def to_chunks(t):
        return t.reshape(bsz, n, c, h, -1).transpose(0, 3, 1, 2, 4)

    q, k, v = to_chunks(q), to_chunks(k), to_chunks(v)
    g = jnp.cumsum(g.astype(jnp.float32).reshape(bsz, n, c, h).transpose(0, 3, 1, 2), axis=-1)
    beta = beta.astype(jnp.float32).reshape(bsz, n, c, h).transpose(0, 3, 1, 2)
    tril = jnp.tril(jnp.ones((c, c), dtype=bool))
    strict = jnp.tril(jnp.ones((c, c), dtype=bool), -1)
    diff = g[..., :, None] - g[..., None, :]
    decay = jnp.where(tril, jnp.exp(jnp.where(tril, diff, 0.0)), 0.0)
    kb = k * beta[..., None]
    vb = v * beta[..., None]
    lower = jnp.where(strict, jnp.einsum('bhnid,bhnjd->bhnij', kb, k) * decay, 0.0)
    eye = jnp.eye(c, dtype=jnp.float32)
    a_mat = eye + lower
    t_mat = lax.linalg.triangular_solve(a_mat, jnp.broadcast_to(eye, a_mat.shape), left_side=True,
                                        lower=True, unit_diagonal=True)
    u = t_mat @ vb
    w = t_mat @ (kb * jnp.exp(g)[..., None])
    qk = jnp.where(tril, jnp.einsum('bhnid,bhnjd->bhnij', q, k) * decay, 0.0)

    def step(state, inp):
        q_c, k_c, u_c, w_c, g_c, qk_c = inp
        v_new = u_c - w_c @ state
        o = (q_c * jnp.exp(g_c)[..., None]) @ state + qk_c @ v_new
        g_last = g_c[..., -1]
        k_dec = k_c * jnp.exp(g_last[..., None] - g_c)[..., None]
        state = state * jnp.exp(g_last)[..., None, None] + jnp.einsum('bhcd,bhce->bhde', k_dec, v_new)
        return state, o

    xs = tuple(jnp.moveaxis(t, 2, 0) for t in (q, k, u, w, g, qk))
    state0 = jnp.zeros((bsz, h, dk, dv), jnp.float32)
    _, o = lax.scan(step, state0, xs)
    return o.transpose(1, 0, 3, 2, 4).reshape(bsz, s_len, h, dv)

def gdn_group(qkv, z, a, b, conv_w, a_log, dt_bias, out_norm):
    bsz, s_len, _ = qkv.shape
    qkv = jax.nn.silu(causal_depthwise_conv(qkv, conv_w))
    q, k, v = split_cols(qkv, [GDN_HEADS * GDN_DK, GDN_HEADS * GDN_DK, GDN_HEADS * GDN_DV])
    q = l2norm(q.reshape(bsz, s_len, GDN_HEADS, GDN_DK))
    k = l2norm(k.reshape(bsz, s_len, GDN_HEADS, GDN_DK))
    v = v.reshape(bsz, s_len, GDN_HEADS, GDN_DV)
    beta = jax.nn.sigmoid(b.astype(jnp.float32))
    g = -jnp.exp(a_log.astype(jnp.float32)) * jax.nn.softplus(a.astype(jnp.float32) + dt_bias.astype(jnp.float32))
    o = gated_delta_chunked(q, k, v, g, beta)
    o = rmsnorm(o, out_norm) * jax.nn.silu(z.reshape(bsz, s_len, GDN_HEADS, GDN_DV).astype(jnp.float32))
    return o.reshape(bsz, s_len, GDN_HEADS * GDN_DV).astype(qkv.dtype)

def compress_tokens(t, pe, w1, w2):
    bsz, s_len, g, dh = t.shape
    n_cmp = (s_len - CMP_BLOCK) // CMP_STRIDE + 1
    idx = jnp.arange(n_cmp)[:, None] * CMP_STRIDE + jnp.arange(CMP_BLOCK)[None, :]
    blocks = t[:, idx] + pe[None, None, :, None, :]
    flat = blocks.transpose(0, 1, 3, 2, 4).reshape(bsz, n_cmp, g, CMP_BLOCK * dh)
    return jax.nn.silu(flat @ w1) @ w2

def nsa_group(q, kv_cmp, kv_slc, kv_win, gate_logits, pe_k, w1_k, w2_k, pe_v, w1_v, w2_v):
    bsz, s_len, _ = q.shape
    g_n, hpg, dh = NSA_KV, NSA_HEADS // NSA_KV, NSA_DH
    scale = dh ** -0.5
    pos = jnp.arange(s_len)
    q = q.reshape(bsz, s_len, NSA_HEADS, dh)

    def kv_split(t):
        t = t.reshape(bsz, s_len, 2, g_n, dh)
        return t[:, :, 0], t[:, :, 1]

    k_c, v_c = kv_split(kv_cmp)
    k_s, v_s = kv_split(kv_slc)
    k_w, v_w = kv_split(kv_win)
    q_plain = q.reshape(bsz, s_len, g_n, hpg, dh)
    q_rot = partial_rope(q, pos).reshape(bsz, s_len, g_n, hpg, dh)
    k_s = partial_rope(k_s, pos)
    k_w = partial_rope(k_w, pos)

    kc = compress_tokens(k_c, pe_k, w1_k, w2_k)
    vc = compress_tokens(v_c, pe_v, w1_v, w2_v)
    n_cmp = kc.shape[1]
    s_cmp = jnp.einsum('bsghd,bngd->bghsn', q_plain, kc) * scale
    cmp_start = jnp.arange(n_cmp) * CMP_STRIDE
    p_cmp = masked_softmax(s_cmp, (cmp_start + CMP_BLOCK - 1)[None, :] <= pos[:, None])
    o_cmp = jnp.einsum('bghsn,bngd->bsghd', p_cmp, vc.astype(jnp.float32))

    nb = s_len // SEL_BLOCK
    sel_start = jnp.arange(nb) * SEL_BLOCK
    overlap = ((cmp_start[:, None] < sel_start[None, :] + SEL_BLOCK)
               & (cmp_start[:, None] + CMP_BLOCK > sel_start[None, :])).astype(jnp.float32)
    imp = jnp.einsum('bghsn,nj->bgsj', p_cmp, overlap)
    blk = jnp.arange(nb)[None, :]
    cur = (pos // SEL_BLOCK)[:, None]
    forced = (blk == 0) | (blk == cur) | (blk == cur - 1)
    score = jnp.where(blk <= cur, jnp.where(forced, BIG, imp), NEG)
    n_sel = min(SEL_TOPK, nb)
    _, top_idx = lax.top_k(score, n_sel)

    kb = k_s.reshape(bsz, nb, SEL_BLOCK, g_n, dh).transpose(0, 3, 1, 2, 4)
    vb = v_s.reshape(bsz, nb, SEL_BLOCK, g_n, dh).transpose(0, 3, 1, 2, 4)
    bi = jnp.arange(bsz)[:, None, None, None]
    gi = jnp.arange(g_n)[None, :, None, None]

    def sel_chunk(ci):
        s0 = ci * SEL_QCHUNK
        q_c = lax.dynamic_slice_in_dim(q_rot, s0, SEL_QCHUNK, axis=1)
        idx_c = lax.dynamic_slice_in_dim(top_idx, s0, SEL_QCHUNK, axis=2)
        t_c = s0 + jnp.arange(SEL_QCHUNK)
        kk = kb[bi, gi, idx_c]
        vv = vb[bi, gi, idx_c]
        s = jnp.einsum('bqghd,bgqnkd->bghqnk', q_c, kk) * scale
        key_pos = idx_c[..., None] * SEL_BLOCK + jnp.arange(SEL_BLOCK)
        mask = (key_pos <= t_c[None, None, :, None, None]).reshape(bsz, g_n, 1, SEL_QCHUNK, n_sel * SEL_BLOCK)
        p = masked_softmax(s.reshape(bsz, g_n, hpg, SEL_QCHUNK, n_sel * SEL_BLOCK), mask)
        p = p.reshape(bsz, g_n, hpg, SEL_QCHUNK, n_sel, SEL_BLOCK)
        return jnp.einsum('bghqnk,bgqnkd->bqghd', p, vv.astype(jnp.float32))

    o_slc = lax.map(sel_chunk, jnp.arange(s_len // SEL_QCHUNK))
    o_slc = jnp.moveaxis(o_slc, 0, 1).reshape(bsz, s_len, g_n, hpg, dh)

    kp = jnp.pad(k_w, ((0, 0), (WINDOW, 0), (0, 0), (0, 0)))
    vp = jnp.pad(v_w, ((0, 0), (WINDOW, 0), (0, 0), (0, 0)))

    def win_block(ci):
        s0 = ci * WIN_QBLOCK
        q_c = lax.dynamic_slice_in_dim(q_rot, s0, WIN_QBLOCK, axis=1)
        k_c2 = lax.dynamic_slice_in_dim(kp, s0, WINDOW + WIN_QBLOCK, axis=1)
        v_c2 = lax.dynamic_slice_in_dim(vp, s0, WINDOW + WIN_QBLOCK, axis=1)
        t_c = s0 + jnp.arange(WIN_QBLOCK)
        s_pos = s0 - WINDOW + jnp.arange(WINDOW + WIN_QBLOCK)
        mask = (s_pos[None, :] >= 0) & (s_pos[None, :] <= t_c[:, None]) & (t_c[:, None] - s_pos[None, :] < WINDOW)
        s = jnp.einsum('bqghd,bkgd->bghqk', q_c, k_c2) * scale
        p = masked_softmax(s, mask)
        return jnp.einsum('bghqk,bkgd->bqghd', p, v_c2.astype(jnp.float32))

    o_win = lax.map(win_block, jnp.arange(s_len // WIN_QBLOCK))
    o_win = jnp.moveaxis(o_win, 0, 1).reshape(bsz, s_len, g_n, hpg, dh)

    gates = jax.nn.sigmoid(gate_logits.astype(jnp.float32)).reshape(bsz, s_len, g_n, hpg, 3)
    o = gates[..., 0:1] * o_cmp + gates[..., 1:2] * o_slc + gates[..., 2:3] * o_win
    return o.reshape(bsz, s_len, NSA_HEADS * dh).astype(q.dtype)

def hybrid_mixer(h, w_in, gdn_conv_w, gdn_a_log, gdn_dt_bias, gdn_out_norm,
                 pe_k, w1_k, w2_k, pe_v, w1_v, w2_v, w_out):
    y = h @ w_in
    (g_qkv, g_z, g_a, g_b, n_q, n_kvc, n_kvs, n_kvw, n_gate) = split_cols(
        y, [W_GDN_QKV, W_GDN_Z, W_GDN_A, W_GDN_B, W_NSA_Q, W_NSA_KV, W_NSA_KV, W_NSA_KV, W_NSA_GATE])
    o_gdn = gdn_group(g_qkv, g_z, g_a, g_b, gdn_conv_w, gdn_a_log, gdn_dt_bias, gdn_out_norm)
    o_nsa = nsa_group(n_q, n_kvc, n_kvs, n_kvw, n_gate, pe_k, w1_k, w2_k, pe_v, w1_v, w2_v)
    return jnp.concatenate([o_gdn, o_nsa], axis=-1) @ w_out

def setup_inputs(seed: int = 0) -> dict:
    key = jax.random.key(seed)
    ks = jax.random.split(key, 24)
    f32 = jnp.float32

    def nrm(k, shape, scale):
        return jax.random.normal(k, shape, f32) * scale

    def gain(k, shape):
        return 1.0 + 0.02 * jax.random.normal(k, shape, f32)

    dt = jnp.exp(jax.random.uniform(ks[9], (DEPTH, GDN_HEADS), f32) * (jnp.log(0.1) - jnp.log(0.001)) + jnp.log(0.001))
    return {
        "x": jax.random.normal(ks[0], (BATCH, SEQ, D_MODEL), f32),
        "ffn1_norm": gain(ks[1], (DEPTH, D_MODEL)),
        "ffn1_w_gate": nrm(ks[2], (DEPTH, D_MODEL, D_FF), D_MODEL ** -0.5),
        "ffn1_w_up": nrm(ks[3], (DEPTH, D_MODEL, D_FF), D_MODEL ** -0.5),
        "ffn1_w_down": nrm(ks[4], (DEPTH, D_FF, D_MODEL), D_FF ** -0.5),
        "mix_norm": gain(ks[5], (DEPTH, D_MODEL)),
        "w_in": nrm(ks[6], (DEPTH, D_MODEL, D_IN), D_MODEL ** -0.5),
        "gdn_conv_w": nrm(ks[7], (DEPTH, GDN_CONV, W_GDN_QKV), GDN_CONV ** -0.5),
        "gdn_a_log": jnp.log(jax.random.uniform(ks[8], (DEPTH, GDN_HEADS), f32, 1.0, 16.0)),
        "gdn_dt_bias": dt + jnp.log(-jnp.expm1(-dt)),
        "gdn_out_norm": gain(ks[10], (DEPTH, GDN_DV)),
        "cmp_pe_k": nrm(ks[11], (DEPTH, CMP_BLOCK, NSA_DH), 0.1),
        "cmp_w1_k": nrm(ks[12], (DEPTH, CMP_BLOCK * NSA_DH, CMP_HIDDEN), (CMP_BLOCK * NSA_DH) ** -0.5),
        "cmp_w2_k": nrm(ks[13], (DEPTH, CMP_HIDDEN, NSA_DH), CMP_HIDDEN ** -0.5),
        "cmp_pe_v": nrm(ks[14], (DEPTH, CMP_BLOCK, NSA_DH), 0.1),
        "cmp_w1_v": nrm(ks[15], (DEPTH, CMP_BLOCK * NSA_DH, CMP_HIDDEN), (CMP_BLOCK * NSA_DH) ** -0.5),
        "cmp_w2_v": nrm(ks[16], (DEPTH, CMP_HIDDEN, NSA_DH), CMP_HIDDEN ** -0.5),
        "w_out": nrm(ks[17], (DEPTH, D_MIX, D_MODEL), D_MIX ** -0.5),
        "ffn2_norm": gain(ks[18], (DEPTH, D_MODEL)),
        "ffn2_w_gate": nrm(ks[19], (DEPTH, D_MODEL, D_FF), D_MODEL ** -0.5),
        "ffn2_w_up": nrm(ks[20], (DEPTH, D_MODEL, D_FF), D_MODEL ** -0.5),
        "ffn2_w_down": nrm(ks[21], (DEPTH, D_FF, D_MODEL), D_FF ** -0.5),
        "final_norm": gain(ks[22], (D_MODEL,)),
    }

def reference(x, ffn1_norm, ffn1_w_gate, ffn1_w_up, ffn1_w_down, mix_norm, w_in,
              gdn_conv_w, gdn_a_log, gdn_dt_bias, gdn_out_norm,
              cmp_pe_k, cmp_w1_k, cmp_w2_k, cmp_pe_v, cmp_w1_v, cmp_w2_v, w_out,
              ffn2_norm, ffn2_w_gate, ffn2_w_up, ffn2_w_down, final_norm):
    for l in range(DEPTH):
        h = rmsnorm(x, ffn1_norm[l])
        x = x + 0.5 * swiglu(h, ffn1_w_gate[l], ffn1_w_up[l], ffn1_w_down[l])
        h = rmsnorm(x, mix_norm[l])
        x = x + hybrid_mixer(h, w_in[l], gdn_conv_w[l], gdn_a_log[l], gdn_dt_bias[l], gdn_out_norm[l],
                             cmp_pe_k[l], cmp_w1_k[l], cmp_w2_k[l], cmp_pe_v[l], cmp_w1_v[l], cmp_w2_v[l],
                             w_out[l])
        h = rmsnorm(x, ffn2_norm[l])
        x = x + 0.5 * swiglu(h, ffn2_w_gate[l], ffn2_w_up[l], ffn2_w_down[l])
    return rmsnorm(x, final_norm)


_drawn_inputs = setup_inputs


def setup_inputs(seed=0):
    import zlib

    import numpy as np

    out = dict(_drawn_inputs(seed))
    spreads = {}
    factors = {'ffn1_norm': 5.504,
     'mix_norm': 3.997,
     'gdn_out_norm': 6.431,
     'cmp_pe_k': 8.0,
     'cmp_pe_v': 25.089,
     'ffn2_norm': 7.949,
     'final_norm': 7.972}
    for name, (base, spread) in spreads.items():
        noise = np.random.default_rng([zlib.crc32(name.encode()), seed]).standard_normal(out[name].shape)
        drawn = base * np.exp(spread * noise) if base else spread * noise
        out[name] = __import__('jax').numpy.asarray(drawn.astype(out[name].dtype))
    for name, factor in factors.items():
        out[name] = (out[name] * factor).astype(out[name].dtype)
    return out
```

```python
from contextlib import ExitStack

import concourse.bass as bass
from concourse import mybir
from concourse.alu_op_type import AluOpType as ALU

ACT = mybir.ActivationFunctionType
F32 = mybir.dt.float32
F32R = mybir.dt.float32r
BF16 = mybir.dt.bfloat16
AX_X = mybir.AxisListType.X

P = 128
SEQ = 512
D_MODEL = 1024
KT = D_MODEL // P
TT = SEQ // P
D_FF = 2816
FT = D_FF // P
HALVES = (12, 10)
EPS = 1e-6
NEG = -1e30

GDN_HEADS, GDN_DK, CONV_TAPS, CHUNK = 4, 128, 4, 64
NSA_HEADS, NSA_KV, NSA_DH = 8, 2, 64
HPG = NSA_HEADS // NSA_KV
CMP_BLOCK, CMP_STRIDE, CMP_HIDDEN = 32, 16, 128
N_CMP = (SEQ - CMP_BLOCK) // CMP_STRIDE + 1
CMP_PAD = 32
SEL_BLOCK, SEL_TOPK, WINDOW = 64, 16, 512
ROPE_THETA, ROPE_DIM = 500000.0, NSA_DH // 4
assert SEQ // SEL_BLOCK <= SEL_TOPK and WINDOW >= SEQ
assert sum(HALVES) == FT and N_CMP < CMP_PAD

CONST_WIDTHS = [("ident", P), ("ones", 2), ("tri", P), ("chunk_ones", P), ("neg_chunk", P), ("neg_causal", P),
                ("levels", 6 * P), ("cos", SEQ), ("sin", SEQ), ("rope_swap", P), ("cmp_valid", TT * CMP_PAD),
                ("cmp_neg", TT * CMP_PAD)]
PARAM_WIDTHS = [("norms", 4 * KT), ("conv_w", 12 * CONV_TAPS), ("out_norm", 1), ("a_log", 4), ("dt_bias", 4),
                ("pe_k", CMP_BLOCK), ("pe_v", CMP_BLOCK), ("w2_k", P), ("w2_v", NSA_DH)]


def columns(widths):
    at, out = 0, {}
    for name, w in widths:
        out[name] = (at, at + w)
        at += w
    return out, at


CONST_AT, CONST_N = columns(CONST_WIDTHS)
PARAM_AT, PARAM_N = columns(PARAM_WIDTHS)

RING = 2
SLOT = 16 * P
FFN_STEPS = FT + 2 * KT
MIX0 = FFN_STEPS
PROJ_STEPS = 14
CMP0 = MIX0 + PROJ_STEPS
CMP_STEPS = 4
OUT0 = CMP0 + CMP_STEPS
OUT_STEPS = 4
FFN2_0 = OUT0 + OUT_STEPS
STEPS = FFN2_0 + FFN_STEPS


def splits(step):
    return step if step <= CMP0 else step - CMP_STEPS


GDN_JOBS = (["k_tok", "v_tok", "g_bc", "rb_bc", "kk", "kq", "c1"]
            + [f"{n}{l}" for l in range(1, 6) for n in ("y", "t", "u") if (n, l) != ("t", 5)]
            + ["uu", "w", "vn0", "s0", "vn1", "o", "s1", "ss"])
NJ = len(GDN_JOBS)
GDN_SEGS = ([["k_tok", "v_tok"], ["g_bc", "rb_bc"], ["kk", "kq"], ["c1"]]
            + [s for l in range(1, 6) for s in (["y%d" % l], ["t%d" % l, "u%d" % l] if l < 5 else ["u5"])]
            + [["uu", "w"], ["vn0"], ["o_0", "s0"], ["vn1"], ["o_1", "s1"], ["ss"]])

UNITS = [(tq, br, h) for tq in range(TT) for br in range(2)
         for j in range(HPG) for h in (j, HPG + j)]
NU = len(UNITS)


def schedule():
    segs = [(tt, s) for tt in range(TT) for s in range(len(GDN_SEGS))]
    out, at = [], 0
    slots = NU + 4
    for i in range(slots):
        n = min(len(segs), (i + 1) * len(segs) // (slots - 4) + 1)
        out.append((i, segs[at:n]))
        at = n
    return out


SCHEDULE = schedule()
FIN_SLOT = {16 * (tq + 1) + 3: tq for tq in range(TT)}


def pt_order():
    order = []
    for i in range(NU + 4):
        if 1 <= i <= NU:
            order.append(("unit", i - 1))
        if i % 16 == 0 and i > 0:
            order.append(("cmp", i // 16 - 1))
        if i in FIN_SLOT:
            order.append(("fin", FIN_SLOT[i]))
    return dict(zip(order, [None] + order[:-1]))


PT_BEFORE = pt_order()


def turns(eng, n, body, peel_first=0, peel_last=0):
    for i in range(peel_first):
        body(i)
    if n - peel_last > peel_first:
        with eng.Fori(peel_first, n - peel_last) as i:
            body(i)
    for i in range(n - peel_last, n):
        body(i)


def positive(v):
    return not (isinstance(v, int) and v <= 0)


def build(nc, dram, out):
    with ExitStack() as ctx:
        def sb(name, cols, dt=F32, side=None, stack=ctx):
            return stack.enter_context(nc.sbuf_tensor(name, [P, cols], dt, side=side) if side
                                       else nc.sbuf_tensor(name, [P, cols], dt))

        def sem(name):
            return ctx.enter_context(nc.semaphore(name))

        x = sb("x", KT * SEQ)[:, :].rearrange("p (k t) -> p k t", k=KT)
        consts = sb("consts", CONST_N)
        params = sb("params", PARAM_N)
        ident_bf = sb("ident_bf", P, BF16)
        neg_causal_bf = sb("neg_causal_bf", P, BF16)
        sq_sum = sb("sq_sum", SEQ)
        sq = sb("sq", 2 * SEQ)[:, :].rearrange("p (b t) -> p b t", b=2)
        h_raw = sb("h_raw", 2 * SEQ)[:, :].rearrange("p (b t) -> p b t", b=2)
        rms = sb("rms", TT)
        eps_col = sb("eps_col", 1)[:, :]
        rstd = sb("rstd", TT)
        raw = sb("raw", RING * SLOT)[:, :].rearrange("p (b n) -> p b n", b=RING)
        h_hi = sb("h_hi", KT * SEQ, F32R)[:, :].rearrange("p (k t) -> p k t", k=KT)
        h_lo = sb("h_lo", KT * SEQ, F32R)[:, :].rearrange("p (k t) -> p k t", k=KT)

        with ExitStack() as ring:
            w_hi = sb("w_hi", RING * SLOT, F32R, "right", ring)[:, :].rearrange("p (b n) -> p b n", b=RING)
            w_lo = sb("w_lo", RING * SLOT, F32R, "right", ring)[:, :].rearrange("p (b n) -> p b n", b=RING)
        gdn_names = ["kbg", "kdec", "vb", "decay", "decay_k", "lt", "qk", "tinv", "uinv", "ysb", "cm0", "cm1",
                     "qe", "usb", "wsb", "egbc"]
        with ExitStack() as ring:
            blocks = sb("blocks", 2 * CMP_BLOCK * 2 * CMP_PAD, F32, "right", ring)[:, :].rearrange(
                "p (c i g n) -> p c i g n", c=2, g=2, n=CMP_PAD)
        B = {}
        for n in gdn_names:
            B[n] = sb(n, SEQ, side="right")[:, :].rearrange("p (h t) -> p h t", h=GDN_HEADS)

        with ExitStack() as ff:
            act_hi = sb("act_hi", HALVES[0] * SEQ, F32R, stack=ff)[:, :].rearrange("p (f t) -> p f t", t=SEQ)
            act_lo = sb("act_lo", HALVES[0] * SEQ, F32R, stack=ff)[:, :].rearrange("p (f t) -> p f t", t=SEQ)
            gate_sb = sb("gate_sb", 2 * SEQ, stack=ff)[:, :].rearrange("p (b t) -> p b t", b=2)
            act_raw = sb("act_raw", 2 * SEQ, stack=ff)[:, :].rearrange("p (b t) -> p b t", b=2)
        kqv = sb("kqv", 12 * SEQ)[:, :].rearrange("p (t s) -> p t s", s=SEQ)
        z = sb("z", GDN_HEADS * SEQ)[:, :].rearrange("p (t s) -> p t s", s=SEQ)
        nq = sb("nq", HPG * SEQ)[:, :].rearrange("p (t s) -> p t s", s=SEQ)
        nq_rot = sb("nq_rot", HPG * SEQ)[:, :].rearrange("p (t s) -> p t s", s=SEQ)
        nk_rot = sb("nk_rot", 2 * SEQ)[:, :].rearrange("p (t s) -> p t s", s=SEQ)
        v_tok = sb("v_tok", TT * 4 * NSA_DH)[:, :].rearrange("p (t n) -> p t n", t=TT)
        PRE = SEQ + CONV_TAPS - 1
        pre = sb("pre", 2 * PRE)[:, :].rearrange("p (b t) -> p b t", b=2)
        cv = sb("cv", 2 * SEQ)[:, :].rearrange("p (b t) -> p b t", b=2)
        small = sb("small", TT * 32)[:, :].rearrange("p (t n) -> p t n", t=TT)
        kc = sb("kc", CMP_PAD)
        hid_t = sb("hid_t", 2 * CMP_HIDDEN)[:, :].rearrange("p (c n) -> p c n", c=2)
        hid_k = sb("hid_k", 2 * CMP_PAD)
        hid_v = sb("hid_v", 2 * P)[:, :].rearrange("p (g n) -> p g n", g=2)
        bdv = sb("bdv", 2 * HPG * NSA_DH)[:, :].rearrange("p (g n) -> p g n", g=2)
        p_cmp_t = sb("p_cmp_t", 2 * P)[:, :].rearrange("p (g t) -> p g t", g=2)
        vnew = sb("vnew", SEQ)[:, :].rearrange("p (h t) -> p h t", h=GDN_HEADS)
        state = sb("state", SEQ)[:, :].rearrange("p (h t) -> p h t", h=GDN_HEADS)
        state_dec = sb("state_dec", SEQ)[:, :].rearrange("p (h t) -> p h t", h=GDN_HEADS)
        neg_g = sb("neg_g", SEQ)[:, :].rearrange("p (h t) -> p h t", h=GDN_HEADS)
        tiny_names = ["apd", "a_abs", "a_exp", "a_ln", "a_max", "g", "eg", "ekd", "rb", "s_kbg", "s_kd", "s_b",
                      "dgl", "ssq", "rqs", "rq2", "vv", "o_rms", "o_rstd", "fac"]
        tiny = {n: sb("t_" + n, 16) for n in tiny_names}
        l2rms, l2r, gcl = sb("l2rms", 32), sb("l2r", 32), sb("gcl", 32)
        ea = sb("ea", 4)
        small_feat = z[:, 3, :]
        sg_exp = sb("sg_exp", TT * 28)[:, :].rearrange("p (t n) -> p t n", t=TT)
        sg = sb("sg", TT * 28)[:, :].rearrange("p (t n) -> p t n", t=TT)
        neg_max = sb("neg_max", 2)
        sums = sb("sums", 2 * TT * NSA_HEADS)
        rsum = sb("rsum", NSA_HEADS)
        fgate = sb("fgate", NSA_HEADS)
        cmp_max, cmp_sum, cmp_f = sb("cmp_max", 32), sb("cmp_sum", 32), sb("cmp_f", 32)
        s_cmp = sb("s_cmp", 2 * TT * HPG * CMP_PAD)[:, :].rearrange(
            "p (g t h n) -> p g t h n", g=2, t=TT, n=CMP_PAD)
        p_att = pre[:, :, 0:SEQ]
        p_att_t = cv
        o_acc = h_raw
        o_tmp = sq

        banks = [ctx.enter_context(nc.psum_tensor(f"bank{i}", [P, SEQ], F32)) for i in range(8)]

        def const(name):
            a, b = CONST_AT[name]
            return consts[:, a:b]

        def param(name):
            a, b = PARAM_AT[name]
            return params[:, a:b]

        ident, tri, ones = const("ident"), const("tri"), const("ones")[:, 0:1]
        level = const("levels").rearrange("p (l n) -> p l n", n=P)
        norm_w = param("norms").rearrange("p (m k) -> p m k", k=KT)
        conv_w = param("conv_w").rearrange("p (t j) -> p t j", j=CONV_TAPS)

        def over(col, n):
            return col.unsqueeze(2).to_broadcast([P, col.shape[1], n])

        def per_head(m, heads=GDN_HEADS):
            return m.unsqueeze(1).to_broadcast([P, heads, m.shape[1]])

        def h4(bank):
            return banks[bank][:, :].rearrange("p (h t) -> p h t", h=4)

        def tcol(name, tt):
            return tiny[name][:, 4 * tt:4 * tt + 4]

        eps_set = sem("eps_set")
        consts_landed = sem("consts_landed")
        rest_landed = sem("rest_landed")
        params_landed = sem("params_landed")
        consts_bf = sem("consts_bf")
        hi_ready = sem("hi_ready")
        lo_ready = sem("lo_ready")
        step_done = sem("step_done")
        silu_ready = sem("silu_ready")
        act_raw_ready = sem("act_raw_ready")
        act_hi_ready = sem("act_hi_ready")
        act_ready = sem("act_ready")
        x_added = sem("x_added")
        sq_ready = sem("sq_ready")
        sum_cleared = sem("sum_cleared")
        sq_summed = sem("sq_summed")
        sq_multiplied = sem("sq_multiplied")
        ss_ready = sem("ss_ready")
        rms_ready = sem("rms_ready")
        rstd_ready = sem("rstd_ready")
        bc_ready = sem("bc_ready")
        h_raw_ready = sem("h_raw_ready")
        h_hi_ready = sem("h_hi_ready")
        h_ready = sem("h_ready")
        y_ready = sem("y_ready")
        out_landed = sem("out_landed")
        small_evac = sem("small_evac")
        proj_evac = sem("proj_evac")
        conv_step = sem("conv_step")
        kqv_ready = sem("kqv_ready")
        kqv_sq = sem("kqv_sq")
        l2_done = sem("l2_done")
        rope_mm = sem("rope_mm")
        rope_a = sem("rope_a")
        rope_b = sem("rope_b")
        rope_ready = sem("rope_ready")
        pads_set = sem("pads_set")
        blocks_zero = sem("blocks_zero")
        blocks_ready = sem("blocks_ready")
        hid_t_ready = sem("hid_t_ready")
        hid_turned = sem("hid_turned")
        hid_ready = sem("hid_ready")
        small_t = sem("small_t")
        small_f = sem("small_f")
        kcvc_mm = sem("kcvc_mm")
        kc_ready = sem("kc_ready")
        bdv_ready = sem("bdv_ready")
        tiny_act = sem("tiny_act")
        tiny_dve = sem("tiny_dve")
        cum_mm = sem("cum_mm")
        gcl_ready = sem("gcl_ready")
        cmp_mm = sem("cmp_mm")
        cmp_dve = sem("cmp_dve")
        cmp_exp = sem("cmp_exp")
        cmp_pt = sem("cmp_pt")
        cmp_pt_evac = sem("cmp_pt_evac")
        cmp_pv = sem("cmp_pv")
        s_done = sem("s_done")
        nmax_ready = sem("nmax_ready")
        exp_done = sem("exp_done")
        pt_done = sem("pt_done")
        pt_evac = sem("pt_evac")
        pv_done = sem("pv_done")
        f_ready = sem("f_ready")
        comb_done = sem("comb_done")
        oacc_ready = sem("oacc_ready")
        fin_t = sem("fin_t")
        ocat_hi = sem("ocat_hi")
        ocat_lo = sem("ocat_lo")
        job_done = sem("job_done")
        neg_g_ready = sem("neg_g_ready")
        k_tok_ready = sem("k_tok_ready")
        v_tok_ready = sem("v_tok_ready")
        darg_ready = sem("darg_ready")
        egbc_ready = sem("egbc_ready")
        decay_ready = sem("decay_ready")
        decay_k_ready = sem("decay_k_ready")
        decay_b_ready = sem("decay_b_ready")
        lt_ready = sem("lt_ready")
        qk_ready = sem("qk_ready")
        qe_ready = sem("qe_ready")
        c_ready = sem("c_ready")
        t_ready = sem("t_ready")
        u_ready = sem("u_ready")
        y_copied = sem("y_copied")
        usb_ready = sem("usb_ready")
        wsb_ready = sem("wsb_ready")
        vnew_ready = sem("vnew_ready")
        sdec_ready = sem("sdec_ready")
        state_ready = sem("state_ready")
        o_ready = sem("o_ready")
        o_sq = sem("o_sq")
        ssq_ready = sem("ssq_ready")
        fin_dve = sem("fin_dve")
        fin_act = sem("fin_act")
        fac_bc = sem("fac_bc")
        zo_ready = sem("zo_ready")
        og_ready = sem("og_ready")
        og_hi = sem("og_hi")
        og_lo = sem("og_lo")
        raw_landed = [sem("raw_landed0"), sem("raw_landed1")]
        x_landed = [sem("x_landed%d" % i) for i in range(KT // 2)]

        def three_pass(pe, out_ap, wh, wl, xh, xl, first, last):
            pe.matmul(out_ap, wh, xh, start=first, stop=False)
            pe.matmul(out_ap, wh, xl, start=False, stop=False)
            return pe.matmul(out_ap, wl, xh, start=False, stop=last)

        FF_BASE = (0, FFN2_0)
        X_ADDED0 = (0, 24)
        OUT_ADDED0 = 16

        def halves(f):
            step, n = FF_BASE[f], f * FT
            for half, tiles in enumerate(HALVES):
                yield half, step, tiles, n, X_ADDED0[f] + 8 * half
                step += tiles + KT
                n += tiles

        SUMMED0 = (0, KT // 2, KT // 2 + KT - 1, KT // 2 + 2 * (KT - 1))

        def act_square(act, m, k, par, ready):
            act.wait_ge(*ready)
            if m == 0 and k >= 2:
                if par:
                    act.wait_ge(sq_multiplied, (k - 1) // 2)
                else:
                    act.wait_ge(sq_summed, k // 2)
            elif m:
                act.wait_ge(sq_summed, k + (SUMMED0[m] - 1))
            act.activation(sq[:, par, :], x[:, k, :], ACT.Square).then_inc(sq_ready, 1)

        def pool_clear(pool, m):
            if m:
                pool.wait_ge(ss_ready, m)
            pool.memset(sq_sum[:, :], 0.0).then_inc(sum_cleared, 1)
            pool.wait_ge(sum_cleared, m + 1)

        def pe_norm(pe, m):
            def sum_up(src, first, last):
                for t in range(TT):
                    mm = pe.matmul(banks[6][:, t:t + 1], src[:, t * P:(t + 1) * P], ones,
                                   start=first and t == 0, stop=last and t == TT - 1)
                return mm
            if m == 0:
                pe.wait_ge(consts_landed, 16)
                for k in range(1, KT - 1, 2):
                    pe.wait_ge(sq_ready, k + 1)
                    sum_up(sq[:, 1, :], k == 1, False).then_inc(sq_multiplied, 1)
                pe.wait_ge(sq_summed, KT // 2)
            else:
                pe.wait_ge(sq_summed, SUMMED0[m] + KT - 1)
            sum_up(sq_sum, m > 0, False)
            pe.wait_ge(sq_ready, KT * (m + 1))
            mm = sum_up(sq[:, 1, :], False, True)
            mm.then_inc(ss_ready, 1)
            pe.wait_ge(rstd_ready, m + 1)
            for t in range(TT):
                mm = pe.matmul(banks[7][:, t * P:(t + 1) * P], rstd[:, t:t + 1].to_broadcast([P, P]), ident,
                               start=True, stop=True)
            mm.then_inc(bc_ready, 1)

        def act_rms(act, m):
            act.wait_ge(ss_ready, m + 1)
            if m == 0:
                act.wait_ge(eps_set, 1)
            act.activation(rms[:, :], banks[6][:, 0:TT], ACT.Sqrt, scale=1.0 / D_MODEL,
                           bias=eps_col).then_inc(rms_ready, 1)

        def act_h_hi(act, m):
            for k in range(KT):
                act.wait_ge(h_raw_ready, m * KT + k + 1)
                act.activation(h_hi[:, k, :], h_raw[:, k % 2, :], ACT.Copy).then_inc(h_hi_ready, 1)

        def dve_rstd(dve, m):
            dve.wait_ge(rms_ready, m + 1)
            dve.reciprocal(rstd[:, :], rms[:, :]).then_inc(rstd_ready, 1)
            dve.wait_ge(bc_ready, m + 1)

        def dve_h(dve, m):
            dve_rstd(dve, m)
            if m == 0:
                dve.wait_ge(params_landed, 16)

            def lo(k):
                dve.wait_ge(h_hi_ready, m * KT + k + 1)
                dve.tensor_tensor(h_lo[:, k, :], h_raw[:, k % 2, :], h_hi[:, k, :].bitcast(F32),
                                  ALU.subtract).then_inc(h_ready, 1)
            for k in range(KT):
                if k >= 2:
                    dve.wait_ge(h_ready, m * KT + k - 1)
                dve.scalar_tensor_tensor(h_raw[:, k % 2, :], x[:, k, :], norm_w[:, m, k:k + 1], banks[7][:, :],
                                         ALU.mult, ALU.mult).then_inc(h_raw_ready, 1)
                if k:
                    lo(k - 1)
            lo(KT - 1)

        def pe_ffn(pe, f):
            m = 0 if f == 0 else 2
            for half, step0, tiles, n0, d0 in halves(f):
                down0 = step0 + tiles

                def gate_up(i):
                    for par in range(2):
                        pe.wait_ge(lo_ready, i * 2 + (splits(step0) + par + 1))
                        free = i * 2 + (n0 + par - 1)
                        if positive(free):
                            pe.wait_ge(act_raw_ready, free)
                        for u in range(2):
                            for k in range(KT):
                                if half == 0 and par == 0 and u == 0:
                                    pe.wait_ge(h_ready, m * KT + k + 1)
                                w = slice((u * KT + k) * P, (u * KT + k + 1) * P)
                                mm = three_pass(pe, banks[2 * u + par][:, :], w_hi[:, par, w], w_lo[:, par, w],
                                                h_hi[:, k, :], h_lo[:, k, :], k == 0, k == KT - 1)
                        mm.then_inc(step_done, 1)
                turns(pe, tiles // 2, gate_up, peel_first=int(f == 0 and half == 0))

                def down(i):
                    for par in range(2):
                        pe.wait_ge(lo_ready, i * 2 + (splits(down0) + par + 1))
                        free = i * 2 + (d0 + par - 1)
                        if positive(free):
                            pe.wait_ge(x_added, free)
                        for j in range(tiles):
                            if par == 0 and j in (tiles - 2, tiles - 1):
                                pe.wait_ge(act_ready, n0 + j + 1)
                            w = slice(j * P, (j + 1) * P)
                            mm = three_pass(pe, banks[4 + par][:, :], w_hi[:, par, w], w_lo[:, par, w],
                                            act_hi[:, j, :], act_lo[:, j, :], j == 0, j == tiles - 1)
                        mm.then_inc(step_done, 1)
                turns(pe, KT // 2, down, peel_first=int(f == 0 and half == 0))

        def act_ffn(act, f):
            for half, step0, tiles, n0, d0 in halves(f):
                down0 = step0 + tiles
                last = f == 1 and half == 1

                def gate_up(i):
                    for par in range(2):
                        act.wait_ge(raw_landed[1 - par], i * 16 + 16 * ((step0 + par + 1) // 2 + 1))
                        if positive(i * 2 + (step0 + par)):
                            act.wait_ge(step_done, i * 2 + (step0 + par))
                        act.activation(w_hi[:, 1 - par, :], raw[:, 1 - par, :], ACT.Copy).then_inc(hi_ready, 1)
                        act.wait_ge(step_done, i * 2 + (step0 + par + 1))
                        act.activation(gate_sb[:, par, :], banks[par][:, :], ACT.Silu).then_inc(silu_ready, 1)
                turns(act, tiles // 2, gate_up, peel_first=int(f == 0 and half == 0))

                def down(i):
                    for par in range(2):
                        if not (last and isinstance(i, int) and i * 2 + par == KT - 1):
                            act.wait_ge(raw_landed[1 - par], i * 16 + 16 * ((down0 + par + 1) // 2 + 1))
                            act.wait_ge(step_done, i * 2 + (down0 + par))
                            act.activation(w_hi[:, 1 - par, :], raw[:, 1 - par, :], ACT.Copy)\
                               .then_inc(hi_ready, 1)
                        if half == 1:
                            act_square(act, 1 if f == 0 else 3, i * 2 + par, par,
                                       (x_added, i * 2 + (d0 + par + 1)))
                turns(act, KT // 2, down, peel_last=int(last))

        def dve_ffn(dve, f):
            for half, step0, tiles, n0, d0 in halves(f):
                down0 = step0 + tiles
                last = f == 1 and half == 1

                def split_next(i, par, base):
                    dve.wait_ge(hi_ready, i * 2 + (splits(base) + par + 2))
                    dve.tensor_tensor(w_lo[:, 1 - par, :], raw[:, 1 - par, :], w_hi[:, 1 - par, :].bitcast(F32),
                                      ALU.subtract).then_inc(lo_ready, 1)

                def gate_up(i):
                    for par in range(2):
                        split_next(i, par, step0)
                        n = i * 2 + (n0 + par)
                        dve.wait_ge(silu_ready, n + 1)
                        if half and positive(n):
                            dve.wait_ge(step_done, step0)
                        dve.tensor_tensor(act_raw[:, par, :], gate_sb[:, par, :], banks[2 + par][:, :],
                                          ALU.mult).then_inc(act_raw_ready, 1)
                        dve.wait_ge(act_raw_ready, n + 1)
                        dve.tensor_copy(act_hi[:, i * 2 + par, :], act_raw[:, par, :]).then_inc(act_hi_ready, 1)
                        dve.wait_ge(act_hi_ready, n + 1)
                        dve.tensor_tensor(act_lo[:, i * 2 + par, :], act_raw[:, par, :],
                                          act_hi[:, i * 2 + par, :].bitcast(F32),
                                          ALU.subtract).then_inc(act_ready, 1)
                turns(dve, tiles // 2, gate_up)

                def down(i):
                    for par in range(2):
                        if not (last and isinstance(i, int) and i * 2 + par == KT - 1):
                            split_next(i, par, down0)
                        dve.wait_ge(step_done, i * 2 + (down0 + par + 1))
                        dve.scalar_tensor_tensor(x[:, i * 2 + par, :], banks[4 + par][:, :], 0.5,
                                                 x[:, i * 2 + par, :], ALU.mult, ALU.add).then_inc(x_added, 1)
                turns(dve, KT // 2, down, peel_last=int(last))

        def pool_sums(pool, m):
            pool_clear(pool, m)
            if m == 0:
                for i in range(KT // 2):
                    pool.wait_ge(sq_ready, 2 * i + 1)
                    if i:
                        pool.wait_ge(sq_summed, i)
                    pool.tensor_tensor(sq_sum[:, :], sq_sum[:, :], sq[:, 0, :], ALU.add).then_inc(sq_summed, 1)
                return

            def body(i):
                for par in range(2):
                    if isinstance(i, int) and i * 2 + par == KT - 1:
                        continue
                    pool.wait_ge(sq_ready, i * 2 + (m * KT + par + 1))
                    pool.wait_ge(sq_summed, i * 2 + (SUMMED0[m] + par))
                    pool.tensor_tensor(sq_sum[:, :], sq_sum[:, :], sq[:, par, :], ALU.add)\
                        .then_inc(sq_summed, 1)
            turns(pool, KT // 2, body, peel_last=1)

        def sp_ffn(sp, f):
            for half, step0, tiles, n0, d0 in halves(f):
                down0 = step0 + tiles
                gu = dram["gate_up%d" % f]
                down = dram["down%d%d" % (f, half)]

                def load_gu(i):
                    for par in range(2):
                        free = i * 2 + (splits(step0) + par - 1)
                        if positive(free):
                            sp.wait_ge(lo_ready, free)
                        sp.dma_start(raw[:, par, :], gu[i * 2 + (n0 - f * FT + par), :, :])\
                          .then_inc(raw_landed[par], 16)
                turns(sp, tiles // 2, load_gu, peel_first=int(f == 0 and half == 0))

                def load_down(i):
                    for par in range(2):
                        sp.wait_ge(lo_ready, i * 2 + (splits(down0) + par - 1))
                        sp.dma_start(raw[:, par, 0:tiles * P], down[i * 2 + par, :, :])\
                          .then_inc(raw_landed[par], 16)
                turns(sp, KT // 2, load_down)

        def slot_w(par, t):
            w = slice(t * P, (t + 1) * P)
            return w_hi[:, par, w], w_lo[:, par, w]

        def half_of(ap3, g):
            return ap3[g * NSA_DH:(g + 1) * NSA_DH]

        KIND = ["small"] + ["conv"] * 6 + ["cmp"] + ["rope_k"] + ["rope_q"] * 2 + ["v"] + ["z"] * 2

        def rope_source(m, ab):
            if KIND[m] == "rope_k":
                return z[:, ab, :], nk_rot[:, ab, :]
            j = 2 * (m - 9) + ab
            return nq[:, j, :], nq_rot[:, j, :]

        def sp_mixer(sp):
            for m in range(PROJ_STEPS):
                step = MIX0 + m
                sp.wait_ge(lo_ready, step - 1)
                if m == 0:
                    sp.dma_start(raw[:, 0, 0:KT * P], dram["w_small"]).then_inc(raw_landed[0], 16)
                else:
                    sp.dma_start(raw[:, m % 2, :], dram["w_in"][m - 1, :, :]).then_inc(raw_landed[m % 2], 16)
            for c in range(CMP_STEPS):
                if c < RING:
                    sp.wait_ge(lo_ready, CMP0 + c - 1)
                else:
                    sp.wait_ge(step_done, CMP0 + c - 1)
                sp.dma_start(raw[:, c % 2, :], dram["w1"][c, :, :]).then_inc(raw_landed[c % 2], 16)
            for o in range(OUT_STEPS):
                if o < RING:
                    sp.wait_ge(step_done, OUT0 + o - 1)
                else:
                    sp.wait_ge(lo_ready, splits(OUT0 + o) - 1)
                sp.dma_start(raw[:, o % 2, :], dram["w_out"][o, :, :]).then_inc(raw_landed[o % 2], 16)

        def act_split(act, step, cols=SLOT):
            par = step % RING
            act.wait_ge(raw_landed[par], 16 * (step // RING + 1))
            act.wait_ge(step_done, step - 1)
            act.activation(w_hi[:, par, 0:cols], raw[:, par, 0:cols], ACT.Copy).then_inc(hi_ready, 1)

        def dve_split(dve, step, cols=SLOT):
            par = step % RING
            dve.wait_ge(hi_ready, splits(step) + 1)
            dve.tensor_tensor(w_lo[:, par, 0:cols], raw[:, par, 0:cols], w_hi[:, par, 0:cols].bitcast(F32),
                              ALU.subtract).then_inc(lo_ready, 1)

        def pe_projection(pe):
            for m in range(PROJ_STEPS):
                par = m % 2
                pe.wait_ge(lo_ready, MIX0 + m + 1)
                if m == 2:
                    pe.wait_ge(small_f, 1)
                if m >= 3:
                    pe.wait_ge(proj_evac, 2 * (m - 2))
                if KIND[m] == "small":
                    for k in range(KT):
                        pe.wait_ge(h_ready, KT + k + 1)
                        mm = three_pass(pe, banks[0][:, :], *slot_w(par, k), h_hi[:, k, :], h_lo[:, k, :],
                                        k == 0, k == KT - 1)
                elif KIND[m] == "v":
                    for t in range(TT):
                        for k in range(KT):
                            tok, w = slice(t * P, (t + 1) * P), slice(k * 2 * P, (k + 1) * 2 * P)
                            o = banks[2 * (t // 2) + par][:, (t % 2) * 2 * P:(t % 2 + 1) * 2 * P]
                            mm = three_pass(pe, o, h_hi[:, k, tok], h_lo[:, k, tok], w_hi[:, par, w],
                                            w_lo[:, par, w], k == 0, k == KT - 1)
                else:
                    for ab in range(2):
                        for k in range(KT):
                            mm = three_pass(pe, banks[2 * ab + par][:, :], *slot_w(par, ab * KT + k),
                                            h_hi[:, k, :], h_lo[:, k, :], k == 0, k == KT - 1)
                mm.then_inc(step_done, 1)
                if m == 1:
                    pe.wait_ge(small_f, 1)
                    for t in range(TT):
                        mm = pe.transpose(banks[6][:, P + 32 * t:P + 32 * (t + 1)],
                                          small_feat[0:32, t * P:(t + 1) * P], ident[0:32, 0:32])
                    mm.then_inc(small_t, 1)
                if 1 <= m - 1 <= 4:
                    for ab in range(2):
                        t = 2 * (m - 2) + ab
                        pe.wait_ge(kqv_sq, t + 1)
                        for tt in range(TT):
                            col = 2 * P + 16 * (t // 4) + 4 * tt + t % 4
                            mm = pe.matmul(banks[6][:, col:col + 1], sq[:, ab, tt * P:(tt + 1) * P], ones,
                                           start=True, stop=True)
                        mm.then_inc(l2_done, 1)
                if m >= 1 and KIND[m - 1].startswith("rope"):
                    for ab in range(2):
                        r = 2 * (m - 1 - 8) + ab
                        pe.wait_ge(proj_evac, 2 * (m - 2) + ab + 1)
                        if r >= 2:
                            pe.wait_ge(rope_b, r - 1)
                        pe.matmul(banks[4 + ab][:, :], const("rope_swap"), rope_source(m - 1, ab)[0],
                                  start=True, stop=True).then_inc(rope_mm, 1)

        def act_projection(act):
            for m in range(PROJ_STEPS):
                par = m % 2
                act.wait_ge(step_done, MIX0 + m + 1)
                if KIND[m] == "small":
                    act.activation(small_feat[0:32, :], banks[0][0:32, :], ACT.Copy).then_inc(small_f, 1)
                if m == 1:
                    act.wait_ge(small_t, 1)
                    act.activation(small, banks[6][:, P:2 * P].rearrange("p (t n) -> p t n", t=TT),
                                   ACT.Copy).then_inc(small_evac, 1)
                for ab in range(2 if m else 0):
                    t = 2 * (m - 1) + ab
                    bank = banks[2 * ab + par][:, :]
                    if KIND[m] in ("conv", "cmp"):
                        if t >= 2:
                            act.wait_ge(conv_step, CONV_TAPS * (t - 1))
                        if m == 1:
                            act.wait_ge(pads_set, 2)
                        act.activation(pre[:, ab, CONV_TAPS - 1:PRE], bank, ACT.Copy).then_inc(proj_evac, 1)
                    elif KIND[m] == "rope_k":
                        act.activation(z[:, ab, :], bank, ACT.Copy).then_inc(proj_evac, 1)
                    elif KIND[m] == "rope_q":
                        act.activation(nq[:, 2 * (m - 9) + ab, :], bank, ACT.Copy,
                                       scale=NSA_DH ** -0.5).then_inc(proj_evac, 1)
                    elif KIND[m] == "v":
                        act.activation(v_tok[:, 2 * ab:2 * ab + 2, :], bank.rearrange("p (t n) -> p t n", t=2),
                                       ACT.Copy).then_inc(proj_evac, 1)
                    else:
                        act.activation(z[:, 2 * (m - 12) + ab, :], bank, ACT.Silu).then_inc(proj_evac, 1)
                if m + 2 < PROJ_STEPS:
                    act_split(act, MIX0 + m + 2)
                if KIND[m] == "conv":
                    for ab in range(2):
                        t = 2 * (m - 1) + ab
                        act.wait_ge(conv_step, CONV_TAPS * (t + 1))
                        act.activation(kqv[:, t, :], cv[:, ab, :], ACT.Silu).then_inc(kqv_ready, 1)
                        if t < 2 * GDN_HEADS:
                            act.wait_ge(kqv_ready, t + 1)
                            if t >= 2:
                                act.wait_ge(l2_done, t - 1)
                            act.activation(sq[:, ab, :], kqv[:, t, :], ACT.Square).then_inc(kqv_sq, 1)

        def dve_projection(dve):
            for m in range(PROJ_STEPS):
                if m + 2 < PROJ_STEPS:
                    dve_split(dve, MIX0 + m + 2)
                if m == 1:
                    dve.wait_ge(small_evac, 1)
                    dve.tensor_tensor(tiny["apd"][:, :].rearrange("p (t h) -> p t h", t=TT), small[:, :, 0:4],
                                      per_head(param("dt_bias"), TT), ALU.add).then_inc(tiny_dve, 1)
                if KIND[m] == "conv":
                    for ab in range(2):
                        t = 2 * (m - 1) + ab
                        dve.wait_ge(proj_evac, t + 1)
                        if t >= 2:
                            dve.wait_ge(kqv_ready, t - 1)
                        for j in range(CONV_TAPS):
                            tap = pre[:, ab, j:j + SEQ]
                            w = conv_w[:, t, j:j + 1]
                            if j == 0:
                                c = dve.tensor_scalar(cv[:, ab, :], tap, w, None, ALU.mult)
                            else:
                                dve.wait_ge(conv_step, CONV_TAPS * t + j)
                                c = dve.scalar_tensor_tensor(cv[:, ab, :], tap, w, cv[:, ab, :],
                                                             ALU.mult, ALU.add)
                            c.then_inc(conv_step, 1)
                if m >= 1 and KIND[m - 1].startswith("rope"):
                    for ab in range(2):
                        r = 2 * (m - 1 - 8) + ab
                        src, dst = rope_source(m - 1, ab)
                        dve.wait_ge(proj_evac, 2 * (m - 2) + ab + 1)
                        dve.tensor_tensor(dst, src, const("cos"), ALU.mult).then_inc(rope_a, 1)
                        dve.wait_ge(rope_mm, r + 1)
                        if r < 2:
                            dve.wait_ge(kqv_ready, 12)
                        else:
                            dve.wait_ge(rope_ready, r - 1)
                        dve.tensor_tensor(cv[:, ab, :], banks[4 + ab][:, :], const("sin"), ALU.mult)\
                           .then_inc(rope_b, 1)
                        dve.wait_ge(rope_a, r + 1)
                        dve.wait_ge(rope_b, r + 1)
                        dve.tensor_tensor(dst, dst, cv[:, ab, :], ALU.add).then_inc(rope_ready, 1)

        def tt4(ap):
            return ap.rearrange("p (t h) -> p t h", t=TT)

        def act_scalars(act):
            act.wait_ge(l2_done, 8)
            act.activation(l2rms[:, :], banks[6][:, 2 * P:2 * P + 32], ACT.Sqrt, bias=eps_col)\
               .then_inc(tiny_act, 1)
            act.wait_ge(tiny_dve, 1)
            act.activation(tiny["a_abs"][:, :], tiny["apd"][:, :], ACT.Abs).then_inc(tiny_act, 1)
            act.wait_ge(tiny_act, 2)
            act.activation(tiny["a_exp"][:, :], tiny["a_abs"][:, :], ACT.Exp, scale=-1.0).then_inc(tiny_act, 1)
            act.wait_ge(tiny_act, 3)
            act.activation(tiny["a_ln"][:, :], tiny["a_exp"][:, :], ACT.Ln, bias=ones).then_inc(tiny_act, 1)
            act.activation(ea[:, :], param("a_log"), ACT.Exp).then_inc(tiny_act, 1)
            act.activation(sg_exp, small[:, :, 4:32], ACT.Exp, scale=-1.0).then_inc(tiny_act, 1)
            act.wait_ge(gcl_ready, 1)
            act.activation(tiny["eg"][:, :], gcl[:, 0:16], ACT.Exp).then_inc(tiny_act, 1)
            act.wait_ge(tiny_dve, 8)
            act.activation(tiny["ekd"][:, :], tiny["dgl"][:, :], ACT.Exp).then_inc(tiny_act, 1)

        def dve_scalars(dve):
            dve.wait_ge(tiny_act, 1)
            dve.reciprocal(l2r[:, :], l2rms[:, :]).then_inc(tiny_dve, 1)
            dve.tensor_scalar(tiny["a_max"][:, :], tiny["apd"][:, :], 0.0, None, ALU.max).then_inc(tiny_dve, 1)
            dve.wait_ge(tiny_dve, 3)
            dve.wait_ge(tiny_act, 4)
            dve.tensor_tensor(tiny["a_max"][:, :], tiny["a_max"][:, :], tiny["a_ln"][:, :], ALU.add)\
               .then_inc(tiny_dve, 1)
            dve.wait_ge(tiny_dve, 4)
            dve.wait_ge(tiny_act, 5)
            dve.scalar_tensor_tensor(tt4(tiny["g"][:, :]), tt4(tiny["a_max"][:, :]), -1.0, per_head(ea[:, :], TT),
                                     ALU.mult, ALU.mult).then_inc(tiny_dve, 1)
            dve.wait_ge(tiny_act, 6)
            dve.tensor_scalar(sg_exp, sg_exp, 1.0, None, ALU.add).then_inc(tiny_dve, 1)
            dve.wait_ge(tiny_dve, 6)
            dve.reciprocal(sg, sg_exp).then_inc(tiny_dve, 1)
            dve.wait_ge(cum_mm, 1)
            dve.tensor_copy(gcl[:, :], banks[6][:, 288:320]).then_inc(gcl_ready, 1)
            dve.wait_ge(gcl_ready, 1)
            dve.tensor_tensor(tiny["dgl"][:, :], gcl[:, 16:32], gcl[:, 0:16], ALU.subtract)\
               .then_inc(tiny_dve, 1)
            dve.wait_ge(tiny_dve, 7)
            dve.tensor_tensor(tt4(tiny["rb"][:, :]), tt4(l2r[:, 0:16]), sg[:, :, 0:4], ALU.mult)\
               .then_inc(tiny_dve, 1)
            dve.wait_ge(tiny_dve, 9)
            dve.wait_ge(tiny_act, 7)
            dve.tensor_tensor(tiny["s_kbg"][:, :], tiny["rb"][:, :], tiny["eg"][:, :], ALU.mult)\
               .then_inc(tiny_dve, 1)
            dve.wait_ge(tiny_act, 8)
            dve.tensor_tensor(tiny["s_kd"][:, :], l2r[:, 0:16], tiny["ekd"][:, :], ALU.mult)\
               .then_inc(tiny_dve, 1)
            dve.tensor_scalar(tiny["rqs"][:, :], l2r[:, 16:32], GDN_DK ** -0.5, None, ALU.mult)\
               .then_inc(tiny_dve, 1)
            dve.wait_ge(tiny_dve, 12)
            dve.tensor_tensor(tiny["rq2"][:, :], tiny["rqs"][:, :], tiny["rqs"][:, :], ALU.mult)\
               .then_inc(tiny_dve, 1)

        def pe_scalars(pe):
            pe.wait_ge(tiny_dve, 5)
            pe.matmul(banks[6][:, 288:304], tri, tiny["g"][:, :], start=True, stop=True)
            pe.matmul(banks[6][:, 304:320], const("chunk_ones"), tiny["g"][:, :], start=True, stop=True)\
              .then_inc(cum_mm, 1)

        def pe_compress(pe):
            pe.wait_ge(proj_evac, 2 * (PROJ_STEPS - 1))
            for c in range(CMP_STEPS):
                kv, par = c // 2, c % 2
                pe.wait_ge(raw_landed[par], 16 * ((CMP0 + c) // RING + 1))
                if par == 0:
                    pe.wait_ge(blocks_ready, 4 * (kv + 1))
                for i in range(16):
                    mm = pe.matmul(banks[kv][0:2 * CMP_PAD, 0:CMP_HIDDEN],
                                   blocks[:, kv, 16 * par + i].rearrange("p g n -> p (g n)"),
                                   raw[:, par, i * P:(i + 1) * P],
                                   start=(par == 0 and i == 0), stop=(par == 1 and i == 15))
                mm.then_inc(step_done, 1)
                if c == 1:
                    pe_scalars(pe)
            for kv in range(2):
                pe.wait_ge(hid_t_ready, kv + 1)
                pe.transpose(banks[2 + kv][:, 0:2 * CMP_PAD], hid_t[0:2 * CMP_PAD, kv, :],
                             ident[0:2 * CMP_PAD, 0:2 * CMP_PAD]).then_inc(hid_turned, 1)
            pe.wait_ge(hid_ready, 3)
            pe.matmul(banks[0][:, 64:128], param("w2_k"), hid_k[:, :], start=True, stop=True)
            for g in range(2):
                mm = pe.matmul(banks[0][:, 128 + 64 * g:192 + 64 * g],
                               hid_v[:, g, :], param("w2_v"), start=True, stop=True)
            mm.then_inc(kcvc_mm, 1)
            pe.wait_ge(kc_ready, 2)
            for h in range(HPG):
                for t in range(TT):
                    for g in range(2):
                        o = (t * HPG + h) * CMP_PAD
                        mm = pe.matmul(banks[1 + 2 * g][:, o:o + CMP_PAD],
                                       half_of(nq, g)[:, h, t * P:(t + 1) * P], half_of(kc, g)[:, :],
                                       start=True, stop=True)
            mm.then_inc(cmp_mm, 1)

        def act_compress(act):
            for kv in range(2):
                act.wait_ge(step_done, CMP0 + 2 * kv + 2)
                act.activation(hid_t[0:2 * CMP_PAD, kv, :], banks[kv][0:2 * CMP_PAD, 0:CMP_HIDDEN], ACT.Silu)\
                   .then_inc(hid_t_ready, 1)
            act.wait_ge(hid_turned, 1)
            act.activation(hid_k[:, :], banks[2][:, 0:2 * CMP_PAD], ACT.Copy).then_inc(hid_ready, 1)
            act.wait_ge(hid_turned, 2)
            for g in range(2):
                act.activation(hid_v[:, g, :].rearrange("p (h n) -> p h n", h=HPG),
                               per_head(banks[3][:, g * CMP_PAD:(g + 1) * CMP_PAD], HPG), ACT.Copy)\
                   .then_inc(hid_ready, 1)
        def dve_blocks(dve):
            dve.wait_ge(step_done, CMP0)
            dve.wait_ge(proj_evac, 2 * 7)
            for kv in range(2):
                dve.wait_ge(blocks_zero, kv + 1)
                strided = pre[:, kv, CONV_TAPS - 1:PRE].rearrange("p (n i) -> p i n", i=CMP_STRIDE)
                pos = param("pe_k" if kv == 0 else "pe_v")
                for r in range(2):
                    i = slice(r * CMP_STRIDE, (r + 1) * CMP_STRIDE)
                    for g in range(2):
                        rows = slice(g * NSA_DH, (g + 1) * NSA_DH)
                        dve.tensor_tensor(blocks[rows, kv, i, g, 0:N_CMP], strided[rows, :, r:r + N_CMP],
                                          pos[rows, i].unsqueeze(2).to_broadcast([NSA_DH, CMP_STRIDE, N_CMP]),
                                          ALU.add).then_inc(blocks_ready, 1)

        def dve_compress(dve):
            dve.wait_ge(kcvc_mm, 1)
            for g in range(2):
                rows = slice(g * NSA_DH, (g + 1) * NSA_DH)
                dve.tensor_copy(kc[rows, :], banks[0][rows, 64 + g * CMP_PAD:64 + (g + 1) * CMP_PAD])\
                   .then_inc(kc_ready, 1)
            for g in range(2):
                for h in range(HPG):
                    rows = slice(h * CMP_PAD, (h + 1) * CMP_PAD)
                    dve.tensor_copy(bdv[rows, g, h * NSA_DH:(h + 1) * NSA_DH],
                                    banks[0][rows, 128 + 64 * g:192 + 64 * g]).then_inc(bdv_ready, 1)
            dve.wait_ge(cmp_mm, 1)
            neg = const("cmp_neg").rearrange("p (t n) -> p t n", t=TT).unsqueeze(2)\
                .to_broadcast([P, TT, HPG, CMP_PAD])
            for g in range(2):
                bank = banks[1 + 2 * g][:, :].rearrange("p (t h n) -> p t h n", t=TT, h=HPG)
                dve.tensor_tensor(s_cmp[:, g], bank, neg, ALU.add).then_inc(cmp_dve, 1)

        def dve_cmp_softmax(dve, i):
            valid = const("cmp_valid").rearrange("p (t n) -> p t n", t=TT).unsqueeze(2)\
                .to_broadcast([P, TT, HPG, CMP_PAD])
            flat = s_cmp.rearrange("p g t h n -> p (g t h) n")
            if i == 1:
                dve.wait_ge(cmp_dve, 2)
                dve.tensor_reduce(cmp_max[:, :], flat, AX_X, ALU.max).then_inc(cmp_dve, 1)
            elif i == 2:
                dve.wait_ge(cmp_dve, 3)
                dve.tensor_tensor(flat, flat, over(cmp_max[:, :], CMP_PAD), ALU.subtract).then_inc(cmp_dve, 1)
            elif i in (4, 5):
                g = i - 4
                dve.wait_ge(cmp_exp, 1)
                dve.tensor_tensor(s_cmp[:, g], s_cmp[:, g], valid, ALU.mult).then_inc(cmp_dve, 1)
            elif i == 6:
                dve.wait_ge(cmp_dve, 6)
                dve.tensor_reduce(cmp_sum[:, :], flat, AX_X, ALU.add).then_inc(cmp_dve, 1)
            elif i == 7:
                dve.wait_ge(cmp_dve, 7)
                dve.tensor_scalar(cmp_sum[:, :], cmp_sum[:, :], 1e-30, None, ALU.max).then_inc(cmp_dve, 1)
            elif i == 8:
                dve.wait_ge(cmp_dve, 8)
                dve.reciprocal(cmp_f[:, :], cmp_sum[:, :]).then_inc(cmp_dve, 1)
            elif i == 10:
                dve.wait_ge(cmp_dve, 9)
                for g in range(2):
                    f = tt4(cmp_f[:, 16 * g:16 * (g + 1)])
                    dve.tensor_tensor(f, f, gate(slice(0, TT), 0)[:, :, HPG * g:HPG * (g + 1)], ALU.mult)\
                       .then_inc(cmp_dve, 1)

        def gate(t, branch):
            return sg[:, t, 4:28].rearrange("p t (h b) -> p t h b", b=3)[:, :, :, branch]

        def unit(i):
            tq, br, h = UNITS[i]
            return tq, br, h, h // HPG, h % HPG, (tq + 1) * P

        def pt_bank_free(pe, kind, i):
            prev = PT_BEFORE[(kind, i)]
            if prev is None:
                return
            what, n = prev
            pe.wait_ge({"unit": pt_evac, "cmp": cmp_pt_evac, "fin": ocat_lo}[what], n + 1)

        def pe_attention(pe, i):
            if i < NU:
                tq, br, h, g, j, n = unit(i)
                bank = banks[i % 2]
                if i == 0:
                    pe.wait_ge(rope_ready, 6)
                    pe.wait_ge(bdv_ready, 8)
                    pe.wait_ge(consts_bf, 2)
                elif i == 1:
                    pe.wait_ge(cmp_dve, 2)
                else:
                    pe.wait_ge(exp_done, i - 1)
                pe.matmul(bank[:, 0:n], half_of(nq_rot, g)[:, j, tq * P:(tq + 1) * P],
                          half_of(nk_rot, g)[:, br, 0:n], start=True, stop=False)
                pe.matmul(bank[:, n - P:n], ident_bf[:, :], neg_causal_bf[:, :], start=False, stop=True)\
                  .then_inc(s_done, 1)
            if 1 <= i <= NU:
                pe.wait_ge(exp_done, i)
                pt_bank_free(pe, "unit", i - 1)
                for kt in range(unit(i - 1)[0] + 1):
                    c = slice(kt * P, (kt + 1) * P)
                    mm = pe.transpose(banks[2][:, c], p_att[:, (i - 1) % 2, c], ident)
                mm.then_inc(pt_done, 1)
            if 2 <= i < NU + 2:
                tq, br, h, g, j, n = unit(i - 2)
                pe.wait_ge(pt_evac, i - 1)
                if i == 2:
                    pe.wait_ge(cmp_dve, 2)
                elif (i - 2) % 8 == 0:
                    pe.wait_ge(comb_done, 3 * tq + br)
                for kt in range(tq + 1):
                    mm = pe.matmul(banks[3][:, h * NSA_DH:(h + 1) * NSA_DH],
                                   p_att_t[:, i % 2, kt * P:(kt + 1) * P],
                                   v_tok[:, kt, (2 * br + g) * NSA_DH:(2 * br + g + 1) * NSA_DH],
                                   start=(kt == 0), stop=(kt == tq))
                mm.then_inc(pv_done, 1)

        def pe_tile_end(pe, i):
            if i % 16 == 0 and i > 0:
                tq = i // 16 - 1
                if tq == 0:
                    pe.wait_ge(cmp_dve, 6)
                pt_bank_free(pe, "cmp", tq)
                for g in range(2):
                    mm = pe.transpose(banks[2][:, g * P:(g + 1) * P],
                                      s_cmp[:, g, tq].rearrange("p h n -> p (h n)"), ident)
                mm.then_inc(cmp_pt, 1)
            if i % 16 == 1 and i > 16:
                tq = i // 16 - 1
                pe.wait_ge(cmp_pt_evac, tq + 1)
                pe.wait_ge(comb_done, 3 * tq + 2)
                for g in range(2):
                    mm = pe.matmul(banks[3][:, g * 256:(g + 1) * 256], p_cmp_t[:, g, :], bdv[:, g, :],
                                   start=True, stop=True)
                mm.then_inc(cmp_pv, 1)
            if i in FIN_SLOT:
                tq = FIN_SLOT[i]
                pe.wait_ge(oacc_ready, 2 * tq + 2)
                pt_bank_free(pe, "fin", tq)
                for f in range(4):
                    mm = pe.transpose(banks[2][:, f * P:(f + 1) * P], o_acc[:, tq % 2, f * P:(f + 1) * P], ident)
                mm.then_inc(fin_t, 1)

        def act_attention(act, i):
            if i < NU:
                tq, br, h, g, j, n = unit(i)
                act.wait_ge(nmax_ready, i + 1)
                if i >= 2:
                    act.wait_ge(pt_done, i - 1)
                act.activation(p_att[:, i % 2, 0:n], banks[i % 2][:, 0:n], ACT.Exp,
                               bias=neg_max[:, i % 2:i % 2 + 1],
                               accum_out=sums[:, 16 * tq + 8 * br + h:16 * tq + 8 * br + h + 1])\
                   .then_inc(exp_done, 1)
            if 1 <= i <= NU:
                n = unit(i - 1)[5]
                act.wait_ge(pt_done, i)
                if i >= 3:
                    act.wait_ge(pv_done, i - 2)
                act.activation(p_att_t[:, (i - 1) % 2, 0:n], banks[2][:, 0:n], ACT.Copy).then_inc(pt_evac, 1)
            if i == 3:
                act.wait_ge(cmp_dve, 4)
                act.activation(s_cmp, s_cmp, ACT.Exp).then_inc(cmp_exp, 1)
        def act_tile_end(act, i):
            if i % 16 == 0 and i > 0:
                tq = i // 16 - 1
                act.wait_ge(cmp_pt, tq + 1)
                if tq:
                    act.wait_ge(cmp_pv, tq)
                act.activation(p_cmp_t, banks[2][:, 0:2 * P].rearrange("p (g t) -> p g t", g=2), ACT.Copy)\
                   .then_inc(cmp_pt_evac, 1)
            if i in FIN_SLOT:
                tq = FIN_SLOT[i]
                act.wait_ge(fin_t, tq + 1)
                act.activation(h_hi[:, 4:8, tq * P:(tq + 1) * P], h4(2), ACT.Copy).then_inc(ocat_hi, 1)

        def dve_attention(dve, i):
            if i < NU:
                n = unit(i)[5]
                dve.wait_ge(s_done, i + 1)
                if i >= 2:
                    dve.wait_ge(exp_done, i - 1)
                dve.tensor_reduce(neg_max[:, i % 2:i % 2 + 1], banks[i % 2][:, 0:n], AX_X, ALU.max,
                                  negate=True).then_inc(nmax_ready, 1)
            if i >= 9 and (i - 9) % 8 == 0 and (i - 9) // 8 < 2 * TT:
                tq, br = (i - 9) // 16, (i - 9) // 8 % 2
                n = 2 * tq + br
                dve.wait_ge(exp_done, 8 * n + 8)
                dve.reciprocal(rsum[:, :], sums[:, 8 * n:8 * n + 8]).then_inc(f_ready, 1)
                dve.wait_ge(f_ready, 2 * n + 1)
                dve.tensor_tensor(fgate[:, :].unsqueeze(1), rsum[:, :].unsqueeze(1),
                                  gate(slice(tq, tq + 1), br + 1), ALU.mult).then_inc(f_ready, 1)
                dve.wait_ge(f_ready, 2 * n + 2)
                dve.wait_ge(pv_done, 8 * n + 8)
                if br and tq:
                    dve.wait_ge(oacc_ready, 2 * tq - 1)
                if not br and tq >= 2:
                    dve.wait_ge(fin_t, tq - 1)
                o = o_tmp[:, 0, :] if br else o_acc[:, tq % 2, :]
                dve.tensor_tensor(o.rearrange("p (h d) -> p h d", d=NSA_DH),
                                  banks[3][:, :].rearrange("p (h d) -> p h d", d=NSA_DH),
                                  over(fgate[:, :], NSA_DH), ALU.mult).then_inc(comb_done, 1)

        def dve_tile_end(dve, i):
            if i % 16 == 1 and i > 16:
                tq = i // 16 - 1
                dve.wait_ge(cmp_pv, tq + 1)
                if tq == 0:
                    dve.wait_ge(cmp_dve, 11)
                else:
                    dve.wait_ge(oacc_ready, 2 * tq)
                f = cmp_f[:, :].rearrange("p (g t h) -> p g t h", g=2, t=TT)[:, :, tq]
                for g in range(2):
                    c = dve.tensor_tensor(
                        o_tmp[:, 1, g * 256:(g + 1) * 256].rearrange("p (h d) -> p h d", d=NSA_DH),
                        banks[3][:, g * 256:(g + 1) * 256].rearrange("p (h d) -> p h d", d=NSA_DH),
                        over(f[:, g], NSA_DH), ALU.mult)
                c.then_inc(comb_done, 1)
            if i in FIN_SLOT:
                tq = FIN_SLOT[i]
                dve.wait_ge(ocat_hi, tq + 1)
                here = slice(tq * P, (tq + 1) * P)
                dve.tensor_tensor(h_lo[:, 4:8, here], h4(2), h_hi[:, 4:8, here].bitcast(F32), ALU.subtract)\
                   .then_inc(ocat_lo, 1)

        def pool_add(pool, i, b):
            if i > 16 and i % 16 == 1:
                tq = i // 16 - 1
                pool.wait_ge(comb_done, 3 * tq + 2 + b)
                if b:
                    pool.wait_ge(oacc_ready, 2 * tq + 1)
                pool.tensor_tensor(o_acc[:, tq % 2, :], o_acc[:, tq % 2, :], o_tmp[:, b, :], ALU.add)\
                    .then_inc(oacc_ready, 1)

        def job(tt, name):
            return NJ * tt + GDN_JOBS.index(name)

        def gbank(tt, name):
            return 4 + job(tt, name) % 4

        def done(eng, tt, name):
            eng.wait_ge(job_done, job(tt, name) + 1)

        def gdn_bank_free(pe, tt, name):
            q = job(tt, name) - 4
            if q < 0:
                return
            t, n = q // NJ, GDN_JOBS[q % NJ]
            readers = {"k_tok": [(k_tok_ready, 2 * t + 2)], "v_tok": [(v_tok_ready, t + 1)],
                       "g_bc": [(darg_ready, t + 1), (egbc_ready, t + 1)],
                       "rb_bc": [(decay_b_ready, t + 1)], "kk": [(lt_ready, t + 1)],
                       "kq": [(qk_ready, t + 1)], "c1": [(t_ready, 5 * t + 1)],
                       "uu": [(usb_ready, t + 1)], "w": [(wsb_ready, t + 1)],
                       "vn0": [(vnew_ready, 2 * t + 1)], "vn1": [(vnew_ready, 2 * t + 2)],
                       "o": [(o_sq, t + 1)], "s0": [(state_ready, 2 * t + 2)],
                       "s1": [(state_ready, 2 * t + 3)], "ss": [(ssq_ready, t + 1)]}
            for l in range(1, 6):
                readers["y%d" % l] = [(y_copied, 5 * t + l)]
                readers["t%d" % l] = [(t_ready, 5 * t + 1 + l)]
                readers["u%d" % l] = [(u_ready, 6 * t + 1 + l)]
            for which, count in readers[n]:
                pe.wait_ge(which, count)

        def pe_gdn(pe, tt, name):
            here = slice(tt * P, (tt + 1) * P)
            l = int(name[1]) if name[0] in "ytu" and name[1:].isdigit() else 0
            c = int(name[-1]) if name[:2] in ("vn", "o_", "s0", "s1") and name[-1].isdigit() else 0
            ch = slice(c * CHUNK, (c + 1) * CHUNK)
            o = h4(gbank(tt, "o" if name.startswith("o_") else name))
            if name != "o_1":
                gdn_bank_free(pe, tt, "o" if name == "o_0" else name)
            if name == "k_tok" and tt == 0:
                pe.wait_ge(kqv_ready, 12)
                pe.wait_ge(rope_ready, 6)
                pe.wait_ge(gcl_ready, 1)
            waits = {"rb_bc": [(tiny_dve, 9)],
                     "c1": [(c_ready, 6 * tt + 1)],
                     "uu": [(u_ready, 6 * tt + 6), (v_tok_ready, tt + 1)],
                     "w": [(k_tok_ready, 2 * tt + 2)],
                     "vn0": [(wsb_ready, tt + 1), (state_ready, 2 * tt + 1)],
                     "vn1": [(state_ready, 2 * tt + 2)],
                     "o_0": [(qe_ready, tt + 1), (qk_ready, tt + 1), (vnew_ready, 2 * tt + 1)],
                     "o_1": [(vnew_ready, 2 * tt + 2)],
                     "ss": [(o_sq, tt + 1)]}
            if name[0] == "y":
                pe.wait_ge(c_ready, 6 * tt + l + 1)
                pe.wait_ge(t_ready, 5 * tt + l)
            elif l:
                pe.wait_ge(y_copied, 5 * tt + l)
                pe.wait_ge(u_ready, 6 * tt + l)
            for which, count in waits.get(name, []):
                pe.wait_ge(which, count)
            for h in range(GDN_HEADS):
                k_t, q_t, v_t = kqv[:, h, here], kqv[:, 4 + h, here], kqv[:, 8 + h, here]
                scalar = slice(4 * tt + h, 4 * tt + h + 1)
                if name == "k_tok":
                    mm = pe.transpose(o[:, h, :], k_t, ident)
                elif name == "v_tok":
                    mm = pe.transpose(o[:, h, :], v_t, ident)
                elif name == "g_bc":
                    mm = pe.matmul(o[:, h, :], tiny["g"][:, scalar].to_broadcast([P, P]), tri,
                                   start=True, stop=True)
                elif name == "rb_bc":
                    mm = pe.matmul(o[:, h, :], tiny["rb"][:, scalar].to_broadcast([P, P]), ident,
                                   start=True, stop=True)
                elif name == "kk":
                    mm = pe.matmul(o[:, h, :], k_t, k_t, start=True, stop=True)
                elif name == "kq":
                    mm = pe.matmul(o[:, h, :], k_t, q_t, start=True, stop=True)
                elif name == "c1":
                    mm = pe.transpose(o[:, h, :], B["cm0"][:, h, :], ident)
                elif name[0] == "y":
                    mm = pe.matmul(o[:, h, :], B["cm%d" % (l % 2)][:, h, :], B["tinv"][:, h, :],
                                   start=True, stop=True)
                elif l and name[0] == "t":
                    mm = pe.matmul(o[:, h, :], B["uinv"][:, h, :], B["ysb"][:, h, :], start=True, stop=True)
                elif l:
                    mm = pe.matmul(o[:, h, :], B["ysb"][:, h, :], B["uinv"][:, h, :], start=True, stop=True)
                elif name == "uu":
                    mm = pe.matmul(o[:, h, :], B["uinv"][:, h, :], B["vb"][:, h, :], start=True, stop=True)
                elif name == "w":
                    mm = pe.matmul(o[:, h, :], B["kbg"][:, h, :], B["uinv"][:, h, :], start=True, stop=True)
                elif name[:2] == "vn":
                    mm = pe.matmul(o[ch, h, :], B["wsb"][:, h, ch], state[:, h, :], start=True, stop=True)
                elif name[:2] == "o_":
                    pe.matmul(o[:, h, ch], state[:, h, :], B["qe"][:, h, ch], start=True, stop=False)
                    mm = pe.matmul(o[:, h, ch], vnew[ch, h, :], B["qk"][ch, h, ch], start=False, stop=True)
                elif name in ("s0", "s1"):
                    mm = pe.matmul(o[:, h, :], B["kdec"][ch, h, :], vnew[ch, h, :], start=True, stop=True)
                else:
                    mm = pe.matmul(o[:, 0, h:h + 1], B["ysb"][:, h, :], ones, start=True, stop=True)
            if name != "o_0":
                mm.then_inc(job_done, 1)

        def act_gdn(act, tt, name):
            here = slice(tt * P, (tt + 1) * P)
            if name == "g_bc":
                done(act, tt, name)
                act.wait_ge(darg_ready, tt + 1)
                act.activation(B["egbc"], h4(gbank(tt, name)), ACT.Exp).then_inc(egbc_ready, 1)
                act.activation(B["decay"], B["decay"], ACT.Exp).then_inc(decay_ready, 1)
            elif name[0] == "y":
                done(act, tt, name)
                act.activation(B["ysb"], h4(gbank(tt, name)), ACT.Copy).then_inc(y_copied, 1)
            elif name == "uu":
                done(act, tt, name)
                act.activation(B["usb"], h4(gbank(tt, name)), ACT.Copy).then_inc(usb_ready, 1)
            elif name == "w":
                done(act, tt, name)
                act.activation(B["wsb"], h4(gbank(tt, name)), ACT.Copy).then_inc(wsb_ready, 1)
            elif name == "o_1":
                done(act, tt, "o")
                act.activation(kqv[:, 8:12, here], h4(gbank(tt, "o")), ACT.Copy).then_inc(o_ready, 1)
                act.activation(B["ysb"], h4(gbank(tt, "o")), ACT.Square).then_inc(o_sq, 1)

        def dve_gdn(dve, tt, name):
            b = h4(gbank(tt, name)) if name in GDN_JOBS else None
            if name in ("y1", "y2", "y3", "y4", "y5", "uu", "w", "o_0", "o_1"):
                return
            done(dve, tt, name)
            if name == "k_tok":
                dve.wait_ge(tiny_dve, 11)
                dve.tensor_tensor(B["kbg"], b, over(tcol("s_kbg", tt), P), ALU.mult).then_inc(k_tok_ready, 1)
                dve.tensor_tensor(B["kdec"], b, over(tcol("s_kd", tt), P), ALU.mult).then_inc(k_tok_ready, 1)
            elif name == "v_tok":
                dve.tensor_tensor(B["vb"], b, over(sg[:, tt, 0:4], P), ALU.mult).then_inc(v_tok_ready, 1)
            elif name == "g_bc":
                dve.wait_ge(neg_g_ready, tt + 1)
                dve.tensor_tensor(B["decay"], b, neg_g, ALU.add).then_inc(darg_ready, 1)
            elif name == "rb_bc":
                dve.wait_ge(decay_k_ready, tt + 1)
                dve.tensor_tensor(B["lt"], b, B["decay_k"], ALU.mult).then_inc(decay_b_ready, 1)
            elif name == "kk":
                dve.wait_ge(decay_b_ready, tt + 1)
                dve.tensor_tensor(B["lt"], b, B["lt"], ALU.mult).then_inc(lt_ready, 1)
            elif name == "kq":
                dve.tensor_tensor(B["qk"], b, B["decay_k"], ALU.mult).then_inc(qk_ready, 1)
            elif name == "c1":
                dve.tensor_tensor(B["tinv"], per_head(ident), b, ALU.subtract).then_inc(t_ready, 1)
            elif name[0] == "t":
                dve.wait_ge(t_ready, 5 * tt + int(name[1]))
                dve.tensor_tensor(B["tinv"], B["tinv"], b, ALU.subtract).then_inc(t_ready, 1)
            elif name[0] == "u":
                dve.wait_ge(u_ready, 6 * tt + int(name[1]))
                dve.tensor_tensor(B["uinv"], B["uinv"], b, ALU.subtract).then_inc(u_ready, 1)
            elif name[:2] == "vn":
                ch = slice(int(name[2]) * CHUNK, (int(name[2]) + 1) * CHUNK)
                dve.wait_ge(usb_ready, tt + 1)
                dve.tensor_tensor(vnew[ch], B["usb"][ch], b[ch], ALU.subtract).then_inc(vnew_ready, 1)
            elif name in ("s0", "s1"):
                dve.wait_ge(sdec_ready, 2 * tt + int(name[1]) + 1)
                dve.tensor_tensor(state, state_dec, b, ALU.add).then_inc(state_ready, 1)
            else:
                dve.tensor_copy(tcol("ssq", tt), b[:, 0, 0:4]).then_inc(ssq_ready, 1)

        def pool_gdn(pool, tt, name):
            here = slice(tt * P, (tt + 1) * P)

            def below(l):
                if l == 0:
                    pool.wait_ge(lt_ready, tt + 1)
                if l >= 2:
                    done(pool, tt, "c1" if l == 2 else "y%d" % (l - 2))
                if l == 2:
                    pool.wait_ge(u_ready, 6 * tt + 1)
                pool.tensor_tensor(B["cm%d" % (l % 2)], B["lt"], per_head(level[:, l, :]), ALU.mult)\
                    .then_inc(c_ready, 1)
            if name == "k_tok":
                if tt:
                    pool.wait_ge(darg_ready, tt)
                else:
                    pool.wait_ge(gcl_ready, 1)
                pool.tensor_tensor(neg_g, per_head(const("neg_chunk")), over(gcl[:, 4 * tt:4 * tt + 4], P),
                                   ALU.subtract).then_inc(neg_g_ready, 1)
            elif name == "g_bc":
                pool.wait_ge(egbc_ready, tt + 1)
                pool.tensor_tensor(B["qe"], kqv[:, 4:8, here], B["egbc"], ALU.mult).then_inc(qe_ready, 1)
            elif name == "rb_bc":
                pool.wait_ge(decay_ready, tt + 1)
                pool.tensor_tensor(B["decay_k"], B["decay"], over(l2r[:, 4 * tt:4 * tt + 4], P), ALU.mult)\
                    .then_inc(decay_k_ready, 1)
            elif name == "kk":
                below(0)
                pool.wait_ge(c_ready, 6 * tt + 1)
                pool.tensor_tensor(B["uinv"], per_head(ident), B["cm0"], ALU.subtract).then_inc(u_ready, 1)
                below(1)
            elif name == "c1":
                below(2)
            elif name[0] == "y" and name != "y5" and int(name[1]) + 2 < 6:
                below(int(name[1]) + 2)
            elif name in ("vn0", "vn1"):
                c = int(name[2])
                pool.wait_ge(state_ready, 2 * tt + c + 1)
                last = (c + 1) * CHUNK - 1
                pool.tensor_tensor(state_dec, state, B["egbc"][:, :, last:last + 1].to_broadcast(
                    [P, GDN_HEADS, GDN_DK]), ALU.mult).then_inc(sdec_ready, 1)

        def dve_gdn_end(dve):
            dve.wait_ge(o_ready, TT)
            for h in range(GDN_HEADS):
                dve.scalar_tensor_tensor(z[:, h, :], z[:, h, :], param("out_norm"), kqv[:, 8 + h, :],
                                         ALU.mult, ALU.mult).then_inc(zo_ready, 1)
            dve.wait_ge(ssq_ready, TT)
            dve.tensor_tensor(tiny["vv"][:, :], tiny["ssq"][:, :], tiny["rq2"][:, :], ALU.mult)\
               .then_inc(fin_dve, 1)
            dve.wait_ge(fin_act, 1)
            dve.reciprocal(tiny["o_rstd"][:, :], tiny["o_rms"][:, :]).then_inc(fin_dve, 1)
            dve.wait_ge(fin_dve, 2)
            dve.tensor_tensor(tiny["fac"][:, :], tiny["o_rstd"][:, :], tiny["rqs"][:, :], ALU.mult)\
               .then_inc(fin_dve, 1)
            dve_split(dve, OUT0)
            for h in range(GDN_HEADS):
                dve.wait_ge(fac_bc, h + 1)
                dve.wait_ge(zo_ready, h + 1)
                dve.tensor_tensor(z[:, h, :], z[:, h, :], banks[4 + h][:, :], ALU.mult).then_inc(og_ready, 1)
                if h:
                    dve_og_lo(dve, h - 1)
            dve_og_lo(dve, GDN_HEADS - 1)

        def dve_og_lo(dve, h):
            dve.wait_ge(og_hi, h + 1)
            dve.tensor_tensor(h_lo[:, h, :], z[:, h, :], h_hi[:, h, :].bitcast(F32), ALU.subtract)\
               .then_inc(og_lo, 1)

        def act_gdn_end(act):
            act.wait_ge(fin_dve, 1)
            act.activation(tiny["o_rms"][:, :], tiny["vv"][:, :], ACT.Sqrt, scale=1.0 / GDN_DK, bias=eps_col)\
               .then_inc(fin_act, 1)
            act.wait_ge(job_done, TT * NJ)
            act_split(act, OUT0)
            for h in range(GDN_HEADS):
                act.wait_ge(og_ready, h + 1)
                act.activation(h_hi[:, h, :], z[:, h, :], ACT.Copy).then_inc(og_hi, 1)

        def pe_gdn_end(pe):
            pe.wait_ge(fin_dve, 3)
            pe.wait_ge(state_ready, 2 * TT + 1)
            for h in range(GDN_HEADS):
                for tt in range(TT):
                    c = 4 * tt + h
                    mm = pe.matmul(banks[4 + h][:, tt * P:(tt + 1) * P],
                                   tiny["fac"][:, c:c + 1].to_broadcast([P, P]), ident, start=True, stop=True)
                mm.then_inc(fac_bc, 1)

        def pe_out(pe):
            for o in range(OUT_STEPS):
                par = o % 2
                pe.wait_ge(lo_ready, splits(OUT0 + o) + 1)
                for ab in range(2):
                    if o >= 2:
                        pe.wait_ge(x_added, OUT_ADDED0 + 2 * (o - 2) + ab + 1)
                    for n, k in enumerate([4, 5, 6, 7, 0, 1, 2, 3]):
                        if o == 0 and ab == 0:
                            if k == 4:
                                pe.wait_ge(ocat_lo, TT)
                                pe.wait_ge(og_ready, GDN_HEADS)
                            elif k < 4:
                                pe.wait_ge(og_lo, k + 1)
                        mm = three_pass(pe, banks[4 + 2 * par + ab][:, :], *slot_w(par, ab * KT + k),
                                        h_hi[:, k, :], h_lo[:, k, :], n == 0, n == KT - 1)
                mm.then_inc(step_done, 1)

        def act_out(act):
            for o in range(OUT_STEPS):
                act_split(act, OUT0 + o + 1)
                for ab in range(2):
                    act_square(act, 2, 2 * o + ab, ab, (x_added, OUT_ADDED0 + 2 * o + ab + 1))

        def dve_out(dve):
            for o in range(OUT_STEPS):
                dve_split(dve, OUT0 + o + 1)
                dve.wait_ge(step_done, OUT0 + o + 1)
                for ab in range(2):
                    k = 2 * o + ab
                    dve.tensor_tensor(x[:, k, :], x[:, k, :], banks[4 + 2 * (o % 2) + ab][:, :], ALU.add)\
                       .then_inc(x_added, 1)

        def pe_mixer(pe):
            pe_norm(pe, 1)
            pe_projection(pe)
            pe_compress(pe)
            for i, segs in SCHEDULE:
                pe_attention(pe, i)
                for tt, g in segs:
                    for name in GDN_SEGS[g]:
                        pe_gdn(pe, tt, name)
                pe_tile_end(pe, i)
            pe_gdn_end(pe)
            pe_out(pe)
            pe_norm(pe, 2)

        def act_mixer(act):
            act_split(act, MIX0 + 1)
            act.wait_ge(rest_landed, 16)
            act_rms(act, 1)
            act_h_hi(act, 1)
            act_projection(act)
            act.activation(ident_bf[:, :], ident, ACT.Copy).then_inc(consts_bf, 1)
            act.activation(neg_causal_bf[:, :], const("neg_causal"), ACT.Copy).then_inc(consts_bf, 1)
            act_scalars(act)
            act_compress(act)
            for i, segs in SCHEDULE:
                act_attention(act, i)
                for tt, g in segs:
                    for name in GDN_SEGS[g]:
                        act_gdn(act, tt, name)
                act_tile_end(act, i)
            act_gdn_end(act)
            act_out(act)
            act_rms(act, 2)
            act_h_hi(act, 2)

        def dve_mixer(dve):
            dve_split(dve, MIX0 + 1)
            dve_h(dve, 1)
            dve_projection(dve)
            dve_blocks(dve)
            dve_scalars(dve)
            dve_compress(dve)
            for i, segs in SCHEDULE:
                dve_attention(dve, i)
                dve_cmp_softmax(dve, i)
                for tt, g in segs:
                    for name in GDN_SEGS[g]:
                        dve_gdn(dve, tt, name)
                dve_tile_end(dve, i)
            dve_gdn_end(dve)
            dve_out(dve)
            dve_h(dve, 2)

        def pool_mixer(pool):
            pool.wait_ge(step_done, MIX0)
            pool.memset(pre[:, :, 0:CONV_TAPS - 1], 0.0).then_inc(pads_set, 1)
            pool.memset(bdv, 0.0).then_inc(pads_set, 1)
            pool.memset(state, 0.0).then_inc(state_ready, 1)
            pool.wait_ge(step_done, CMP0)
            for kv in range(2):
                pool.memset(blocks[:, kv], 0.0).then_inc(blocks_zero, 1)
            for i, segs in SCHEDULE:
                pool_add(pool, i, 0)
                for tt, g in segs:
                    for name in GDN_SEGS[g]:
                        pool_gdn(pool, tt, name)
                pool_add(pool, i, 1)


        block = ctx.enter_context(nc.Block())

        @block.sync
        def _(sp):
            for k in range(0, KT, 2):
                sp.dma_start(x[:, k:k + 2, :], dram["x"][:, k:k + 2, :]).then_inc(x_landed[k // 2], 16)
            sp_ffn(sp, 0)
            sp_mixer(sp)
            sp_ffn(sp, 1)
            for k in range(KT):
                sp.wait_ge(y_ready, k + 1)
                sp.dma_start(out[:, k, :], x[:, k, :]).then_inc(out_landed, 16)
            sp.wait_ge(out_landed, 16 * KT)

        @block.gpsimd
        def _(pool):
            pool.memset(eps_col, EPS).then_inc(eps_set, 1)
            pool_sums(pool, 0)
            pool_sums(pool, 1)
            pool_mixer(pool)
            pool_sums(pool, 2)
            pool_sums(pool, 3)

        @block.scalar
        def _(act):
            first = CONST_AT["ones"][1]
            act.dma_start(consts[:, 0:first], dram["consts"][:, 0:first]).then_inc(consts_landed, 16)
            act.dma_start(params[:, :], dram["params"]).then_inc(params_landed, 16)
            for k in range(KT):
                act_square(act, 0, k, k % 2, (x_landed[k // 2], 16))
            act.wait_ge(raw_landed[0], 16)
            act.activation(w_hi[:, 0, :], raw[:, 0, :], ACT.Copy).then_inc(hi_ready, 1)
            act_rms(act, 0)
            act_h_hi(act, 0)
            act.dma_start(consts[:, first:], dram["consts"][:, first:]).then_inc(rest_landed, 16)
            act_ffn(act, 0)
            act_mixer(act)
            act_ffn(act, 1)
            act_rms(act, 3)

        @block.vector
        def _(dve):
            dve.wait_ge(hi_ready, 1)
            dve.tensor_tensor(w_lo[:, 0, :], raw[:, 0, :], w_hi[:, 0, :].bitcast(F32),
                              ALU.subtract).then_inc(lo_ready, 1)
            dve_h(dve, 0)
            dve_ffn(dve, 0)
            dve_mixer(dve)
            dve_ffn(dve, 1)
            dve_rstd(dve, 3)
            for k in range(KT):
                dve.scalar_tensor_tensor(x[:, k, :], x[:, k, :], norm_w[:, 3, k:k + 1], banks[7][:, :],
                                         ALU.mult, ALU.mult).then_inc(y_ready, 1)

        @block.tensor
        def _(pe):
            pe_norm(pe, 0)
            pe_ffn(pe, 0)
            pe_mixer(pe)
            pe_ffn(pe, 1)
            pe_norm(pe, 3)


def shape_constants(np):
    i, j = np.arange(P)[None, :], np.arange(P)[:, None]
    same = (i // CHUNK) == (j // CHUNK)
    c = {"ident": np.eye(P), "tri": same & (j <= i), "chunk_ones": same,
         "neg_chunk": np.where(same & (j <= i), 0.0, NEG), "neg_causal": np.where(i <= j, 0.0, NEG)}
    levels = []
    for l in range(6):
        b = 1 << l
        levels.append((i // (2 * b) == j // (2 * b)) & (i // b % 2 == 1) & (j // b % 2 == 0))
    c["levels"] = np.concatenate(levels, 1)
    half = ROPE_DIM // 2
    inv = np.float32(ROPE_THETA) ** (-np.arange(half, dtype=np.float32) / np.float32(half))
    ang = np.arange(SEQ, dtype=np.float32)[None, :] * inv[:, None]
    cos, sin = np.ones((P, SEQ), np.float32), np.zeros((P, SEQ), np.float32)
    swap = np.zeros((P, P), np.float32)
    for g in (0, NSA_DH):
        for r in range(half):
            cos[g + r], cos[g + half + r] = np.cos(ang[r]), np.cos(ang[r])
            sin[g + r], sin[g + half + r] = np.sin(ang[r]), np.sin(ang[r])
            swap[g + half + r, g + r] = -1.0
            swap[g + r, g + half + r] = 1.0
    c["cos"], c["sin"], c["rope_swap"] = cos, sin, swap
    pos = np.arange(P)[:, None, None] + P * np.arange(TT)[None, :, None]
    n = np.arange(CMP_PAD)[None, None, :]
    valid = (n < N_CMP) & (n * CMP_STRIDE + CMP_BLOCK - 1 <= pos)
    c["cmp_valid"] = valid.reshape(P, -1)
    c["cmp_neg"] = np.where(valid, 0.0, NEG).reshape(P, -1)
    c["ones"] = np.ones((P, 2))
    return np.concatenate([np.asarray(c[k], np.float32) for k, _ in CONST_WIDTHS], 1)


def lay_out(inp, np):
    a = {k: np.asarray(v) for k, v in inp.items()}
    out = {"x": a["x"][0].T.reshape(KT, P, SEQ).transpose(1, 0, 2), "consts": shape_constants(np)}

    def col(v):
        return v.reshape(-1, P).T

    def twice(m):
        return np.concatenate([m, m], 0)
    w2_k = a["cmp_w2_k"][0]
    out["params"] = np.concatenate([
        col(a["ffn1_norm"][0]), col(a["mix_norm"][0]), col(a["ffn2_norm"][0]), col(a["final_norm"]),
        a["gdn_conv_w"][0][:, CONV_ORDER].reshape(CONV_TAPS, 12, P).transpose(2, 1, 0).reshape(P, -1),
        a["gdn_out_norm"][0][:, None], np.repeat(a["gdn_a_log"], P, 0), np.repeat(a["gdn_dt_bias"], P, 0),
        twice(a["cmp_pe_k"][0].T), twice(a["cmp_pe_v"][0].T), np.concatenate([w2_k, w2_k], 1),
        a["cmp_w2_v"][0]], 1)
    for f, name in enumerate(("ffn1", "ffn2")):
        gu = np.stack([a[name + "_w_gate"][0], a[name + "_w_up"][0]])
        out["gate_up%d" % f] = gu.reshape(2, KT, P, FT, P).transpose(3, 2, 0, 1, 4).reshape(FT, P, SLOT)
        row = 0
        for half, tiles in enumerate(HALVES):
            d = a[name + "_w_down"][0][row:row + tiles * P]
            out["down%d%d" % (f, half)] = d.reshape(tiles, P, KT, P).transpose(2, 1, 0, 3).reshape(KT, P, tiles * P)
            row += tiles * P
    w_in = a["w_in"][0]
    tiles = w_in[:, TILE_COLS].reshape(KT, P, 12, 2, P)
    w = tiles.transpose(2, 1, 3, 0, 4).reshape(12, P, SLOT)
    v = w_in[:, V_COLS].reshape(KT, P, 2 * P).transpose(1, 0, 2).reshape(1, P, SLOT)
    out["w_in"] = np.concatenate([w[:10], v, w[10:]], 0)
    w_small = np.zeros((D_MODEL, P), w_in.dtype)
    w_small[:, :32] = w_in[:, SMALL_COLS]
    out["w_small"] = w_small.reshape(KT, P, P).transpose(1, 0, 2).reshape(P, KT * P)
    w1 = np.stack([a["cmp_w1_k"][0], a["cmp_w1_v"][0]]).reshape(2, 2, 16, NSA_DH, CMP_HIDDEN)
    w1 = w1.transpose(0, 1, 3, 2, 4).reshape(CMP_STEPS, NSA_DH, SLOT)
    out["w1"] = np.concatenate([w1, w1], 1)
    out["w_out"] = a["w_out"][0].reshape(KT, P, 4, 2, P).transpose(2, 1, 3, 0, 4).reshape(4, P, SLOT)
    return out


def column_orders():
    hd = GDN_HEADS * GDN_DK
    q0, k0, v0, z0 = 0, hd, 2 * hd, 3 * hd
    a0 = 4 * hd
    nq0 = a0 + 2 * GDN_HEADS
    kvw = 2 * NSA_KV * NSA_DH
    kvc, kvs, kvw0 = nq0 + NSA_HEADS * NSA_DH, nq0 + NSA_HEADS * NSA_DH + kvw, nq0 + NSA_HEADS * NSA_DH + 2 * kvw
    gate0 = kvw0 + kvw
    conv = list(range(k0, k0 + hd)) + list(range(q0, q0 + hd)) + list(range(v0, v0 + hd))
    cols = list(conv)
    cols += list(range(kvc, kvc + 2 * P))
    cols += list(range(kvs, kvs + P)) + list(range(kvw0, kvw0 + P))
    for j in range(HPG):
        for h in (j, HPG + j):
            cols += list(range(nq0 + h * NSA_DH, nq0 + (h + 1) * NSA_DH))
    cols += list(range(z0, z0 + hd))
    v_cols = list(range(kvs + P, kvs + 2 * P)) + list(range(kvw0 + P, kvw0 + 2 * P))
    small = list(range(a0, a0 + 2 * GDN_HEADS)) + list(range(gate0, gate0 + 3 * NSA_HEADS))
    return conv, cols, v_cols, small


CONV_ORDER, TILE_COLS, V_COLS, SMALL_COLS = column_orders()


def kernel(**inputs):
    import numpy as np
    import concourse.bacc as bacc
    from concourse.bass_utils import run_bass_kernel_spmd

    arrays = {k: np.ascontiguousarray(v) for k, v in lay_out(inputs, np).items()}
    nc = bacc.Bacc("TRN2", target_bir_lowering=False, num_devices=1)
    dram = {k: nc.dram_tensor("in_" + k, v.shape, mybir.dt.from_np(v.dtype), kind="ExternalInput").ap()
            for k, v in arrays.items()}
    out = nc.dram_tensor("out_y", (P, KT, SEQ), F32, kind="ExternalOutput").ap()
    build(nc, dram, out)
    r = run_bass_kernel_spmd(nc, [{"in_" + k: v for k, v in arrays.items()}], core_ids=[0])
    y = r.results[0]["out_y"]
    return np.ascontiguousarray(y.transpose(1, 0, 2).reshape(D_MODEL, SEQ).T)[None]
```
